# Optimizing a Trainium2 kernel written in Bass

```python
import math
import jax, jax.numpy as jnp
from jax import lax
import numpy as np

D_MODEL = 1024
BATCH = 1
SEQ = 512
DEPTH = 1

D_MIX = D_MODEL
D_A = D_MIX // 2
A_GROUPS = 4
A_DH = D_A // A_GROUPS
A_CHUNK = 128
D_B = D_MIX - D_A
B_HEADS = 8
B_DH = D_B // B_HEADS
B_BLOCK = 256
B_TOPK = 3
B_QCHUNK = 64
D_IN_PROJ = 2 * D_A + 3 * D_B
D_PLE = 256
N_GROUPS = 4
EXP_PER_GROUP = 8
N_EXPERTS = N_GROUPS * EXP_PER_GROUP
D_FF_EXP = 256
TOP_K_EXP = 2
MOE_TCHUNK = 2048
EPS = 1e-6
NEG = -1e30

kernel_name = "hymba_gmlp_moba_hiermoe_block"

def rms_norm(x, g):
    xf = x.astype(jnp.float32)
    y = xf * lax.rsqrt(jnp.mean(xf * xf, axis=-1, keepdims=True) + EPS)
    return (y * g.astype(jnp.float32)).astype(x.dtype)

def mixer_a(u, v, g_v, w_s, b_s):
    b, s, _ = u.shape
    nc = s // A_CHUNK
    u = jax.nn.gelu(u).reshape(b, nc, A_CHUNK, A_GROUPS, A_DH)
    v = jax.nn.gelu(v).reshape(b, s, A_GROUPS, A_DH)
    v = rms_norm(v, g_v.reshape(A_GROUPS, A_DH)).reshape(b, nc, A_CHUNK, A_GROUPS, A_DH)
    ws = jnp.tril(w_s)
    mixed = jnp.einsum('gts,bnsgd->bntgd', ws, v) + b_s.T[None, None, :, :, None]
    return (u * mixed).reshape(b, s, D_A)

def mixer_b(q, k, v, g_q, g_k):
    b, s, _ = q.shape
    nb = -(-s // B_BLOCK)
    sp = nb * B_BLOCK
    pad = ((0, 0), (0, sp - s), (0, 0))
    q, k, v = (jnp.pad(t, pad).reshape(b, sp, B_HEADS, B_DH).transpose(0, 2, 1, 3) for t in (q, k, v))
    q = rms_norm(q, g_q)
    k = rms_norm(k, g_k)
    scale = 1.0 / math.sqrt(B_DH)
    kb = k.reshape(b, B_HEADS, nb, B_BLOCK, B_DH)
    vb = v.reshape(b, B_HEADS, nb, B_BLOCK, B_DH)
    kmean = jnp.mean(kb.astype(jnp.float32), axis=3)
    gate = jnp.einsum('bhsd,bhnd->bhsn', q.astype(jnp.float32), kmean)
    qblk = jnp.arange(sp) // B_BLOCK
    past = jnp.arange(nb)[None, :] < qblk[:, None]
    gate = jnp.where(past[None, None], gate, NEG)
    k_sel = min(B_TOPK, nb)
    sel_score, sel_idx = lax.top_k(gate, k_sel)
    sel_valid = sel_score > (NEG * 0.5)

    nqc = sp // B_QCHUNK
    q_ch = jnp.moveaxis(q.reshape(b, B_HEADS, nqc, B_QCHUNK, B_DH), 2, 0)
    idx_ch = jnp.moveaxis(sel_idx.reshape(b, B_HEADS, nqc, B_QCHUNK, k_sel), 2, 0)
    val_ch = jnp.moveaxis(sel_valid.reshape(b, B_HEADS, nqc, B_QCHUNK, k_sel), 2, 0)
    gather = jax.vmap(jax.vmap(lambda blocks, ix: blocks[ix]))

    def step(args):
        q_c, idx_c, val_c, c = args
        blk = (c * B_QCHUNK) // B_BLOCK
        k_own = lax.dynamic_index_in_dim(kb, blk, axis=2, keepdims=False)
        v_own = lax.dynamic_index_in_dim(vb, blk, axis=2, keepdims=False)
        k_g = gather(kb, idx_c)
        v_g = gather(vb, idx_c)
        s_g = jnp.einsum('bhqd,bhqnkd->bhqnk', q_c, k_g).astype(jnp.float32) * scale
        s_g = jnp.where(val_c[..., None], s_g, NEG).reshape(b, B_HEADS, B_QCHUNK, k_sel * B_BLOCK)
        s_o = jnp.einsum('bhqd,bhkd->bhqk', q_c, k_own).astype(jnp.float32) * scale
        qpos = c * B_QCHUNK + jnp.arange(B_QCHUNK)
        kpos = blk * B_BLOCK + jnp.arange(B_BLOCK)
        s_o = jnp.where((kpos[None, :] <= qpos[:, None])[None, None], s_o, NEG)
        probs = jax.nn.softmax(jnp.concatenate([s_g, s_o], axis=-1), axis=-1).astype(v.dtype)
        p_g = probs[..., :k_sel * B_BLOCK].reshape(b, B_HEADS, B_QCHUNK, k_sel, B_BLOCK)
        p_o = probs[..., k_sel * B_BLOCK:]
        return (jnp.einsum('bhqnk,bhqnkd->bhqd', p_g, v_g)
                + jnp.einsum('bhqk,bhkd->bhqd', p_o, v_own))

    out = lax.map(step, (q_ch, idx_ch, val_ch, jnp.arange(nqc)))
    out = jnp.moveaxis(out, 0, 2).reshape(b, B_HEADS, sp, B_DH)[:, :, :s]
    return out.transpose(0, 2, 1, 3).reshape(b, s, D_B)

def hier_moe(xn, w_group, w_expert, w_gate_e, w_up_e, w_down_e):
    t = xn.shape[0]
    g_prob = jax.nn.softmax((xn @ w_group).astype(jnp.float32), axis=-1)
    pg, g_sel = lax.top_k(g_prob, 1)
    e_logits = (xn @ w_expert).astype(jnp.float32).reshape(t, N_GROUPS, EXP_PER_GROUP)
    e_in = jnp.take_along_axis(e_logits, g_sel[:, :, None], axis=1)[:, 0]
    e_prob = jax.nn.softmax(e_in, axis=-1)
    e_w, e_idx = lax.top_k(e_prob, TOP_K_EXP)
    e_w = e_w / jnp.sum(e_w, axis=-1, keepdims=True)
    w_in = jnp.sum(jax.nn.one_hot(e_idx, EXP_PER_GROUP, dtype=jnp.float32) * e_w[..., None], axis=1)
    combine = (jax.nn.one_hot(g_sel[:, 0], N_GROUPS, dtype=jnp.float32)[:, :, None]
               * (pg[:, :, None] * w_in[:, None, :])).reshape(t, N_EXPERTS).astype(xn.dtype)

    tc = math.gcd(t, MOE_TCHUNK)
    xs = xn.reshape(t // tc, tc, -1)
    cs = combine.reshape(t // tc, tc, N_EXPERTS)

    def step(args):
        xc, cc = args
        h = jnp.einsum('td,edf->tef', xc, w_gate_e)
        u = jnp.einsum('td,edf->tef', xc, w_up_e)
        a = jax.nn.silu(h) * u * cc[:, :, None]
        return jnp.einsum('tef,efd->td', a, w_down_e)

    return lax.map(step, (xs, cs)).reshape(t, -1)

def setup_inputs(seed: int = 0) -> dict:
    key = jax.random.key(seed)
    ks = jax.random.split(key, 24)
    f = jnp.float32
    nrm = lambda k, shape, s: jax.random.normal(k, shape, f) * s
    gain = lambda k, shape: 1.0 + 0.05 * jax.random.normal(k, shape, f)
    L = DEPTH
    return {
        "x": jax.random.normal(ks[0], (BATCH, SEQ, D_MODEL), f),
        "p": jax.random.normal(ks[1], (DEPTH, BATCH, SEQ, D_PLE), f),
        "g_mix": gain(ks[2], (L, D_MODEL)),
        "w_in": nrm(ks[3], (L, D_MODEL, D_IN_PROJ), D_MODEL ** -0.5),
        "g_v_a": gain(ks[4], (L, D_A)),
        "w_s": nrm(ks[5], (L, A_GROUPS, A_CHUNK, A_CHUNK), A_CHUNK ** -0.5),
        "b_s": 1.0 + 0.1 * jax.random.normal(ks[6], (L, A_GROUPS, A_CHUNK), f),
        "g_q": gain(ks[7], (L, B_DH)),
        "g_k": gain(ks[8], (L, B_DH)),
        "g_out_a": gain(ks[9], (L, D_A)),
        "g_out_b": gain(ks[10], (L, D_B)),
        "w_out": nrm(ks[11], (L, D_MIX, D_MODEL), D_MIX ** -0.5),
        "g_ffn": gain(ks[12], (L, D_MODEL)),
        "w_group": nrm(ks[13], (L, D_MODEL, N_GROUPS), D_MODEL ** -0.5),
        "w_expert": nrm(ks[14], (L, D_MODEL, N_EXPERTS), D_MODEL ** -0.5),
        "w_gate_e": nrm(ks[15], (L, N_EXPERTS, D_MODEL, D_FF_EXP), D_MODEL ** -0.5),
        "w_up_e": nrm(ks[16], (L, N_EXPERTS, D_MODEL, D_FF_EXP), D_MODEL ** -0.5),
        "w_down_e": nrm(ks[17], (L, N_EXPERTS, D_FF_EXP, D_MODEL), D_FF_EXP ** -0.5),
        "g_ple": gain(ks[18], (L, D_MODEL)),
        "w_ple": nrm(ks[19], (L, D_PLE, D_MODEL), D_PLE ** -0.5),
        "w_ple_gate": nrm(ks[20], (L, D_MODEL, D_MODEL), D_MODEL ** -0.5),
    }

def reference(x, p, g_mix, w_in, g_v_a, w_s, b_s, g_q, g_k, g_out_a, g_out_b, w_out,
              g_ffn, w_group, w_expert, w_gate_e, w_up_e, w_down_e, g_ple, w_ple, w_ple_gate):
    b, s, d = x.shape
    h = x
    for i in range(DEPTH):
        xn = rms_norm(h, g_mix[i])
        proj = xn @ w_in[i]
        u_a, v_a, q_b, k_b, v_b = jnp.split(
            proj, [D_A, 2 * D_A, 2 * D_A + D_B, 2 * D_A + 2 * D_B], axis=-1)
        y_a = rms_norm(mixer_a(u_a, v_a, g_v_a[i], w_s[i], b_s[i]), g_out_a[i])
        y_b = rms_norm(mixer_b(q_b, k_b, v_b, g_q[i], g_k[i]), g_out_b[i])
        h = h + jnp.concatenate([y_a, y_b], axis=-1) @ w_out[i]
        hn = rms_norm(h, g_ffn[i]).reshape(b * s, d)
        h = h + hier_moe(hn, w_group[i], w_expert[i], w_gate_e[i], w_up_e[i], w_down_e[i]).reshape(b, s, d)
        gate = jax.nn.sigmoid(rms_norm(h, g_ple[i]) @ w_ple_gate[i])
        h = h + (p[i] @ w_ple[i]) * gate
    return h


_drawn_inputs = setup_inputs


def setup_inputs(seed=0):
    import zlib

    import numpy as np

    out = dict(_drawn_inputs(seed))
    spreads = {}
    factors = {'g_ple': 8.0}
    for name, (base, spread) in spreads.items():
        noise = np.random.default_rng([zlib.crc32(name.encode()), seed]).standard_normal(out[name].shape)
        drawn = base * np.exp(spread * noise) if base else spread * noise
        out[name] = __import__('jax').numpy.asarray(drawn.astype(out[name].dtype))
    for name, factor in factors.items():
        out[name] = (out[name] * factor).astype(out[name].dtype)
    return out
```

```python
import concourse.bass as bass
from concourse import mybir
from contextlib import ExitStack

F32 = mybir.dt.float32
BF16 = mybir.dt.bfloat16
I32 = mybir.dt.int32
U32 = mybir.dt.uint32
ALU = mybir.AluOpType
ACT = mybir.ActivationFunctionType
AX = mybir.AxisListType

P = 128
S = 512
D = 1024
NT = S // P
KD = D // P
DA = 512
GA = 4
H, DH = 8, 64
E, FF = 32, 256
NG, EPG = 4, 8
BLK = 64
RING = 4
PAIRS = 2 * S
EXTRA = (PAIRS - E) // BLK
EXTRA_PAIRS = (EXTRA + 1) // 2
NQ = E // 2 + EXTRA_PAIRS + 1
N_SMALL = 14
EPS = 1e-6
NEG = -1e30
BIG = 3e38
MAGIC = float(0x5F3759DF)


def hybrid_layer(nc, x, p, g_mix, w_in, g_v_a, w_s, b_s, g_q, g_k, g_out_a, g_out_b, w_out, g_ffn,
                 w_group, w_expert, w_gate_e, w_up_e, w_down_e, g_ple, w_ple, w_ple_gate, out):
    x_v = x[0].rearrange("(t p) d -> t p d", p=P)
    out_v = out[0].rearrange("(t p) d -> t p d", p=P)
    p_v = p[0, 0].rearrange("(t p) d -> p t d", p=P)
    win_v = w_in[0].rearrange("(p k) n -> p k n", k=KD)
    wout_v = w_out[0].rearrange("(k p) n -> p k n", p=P)
    wple_v = w_ple[0].rearrange("(k p) n -> p k n", p=P)
    wpg_v = w_ple_gate[0].rearrange("(p k) n -> p (k n)", k=KD)
    gate_v = w_gate_e[0].rearrange("e (p k) f -> e p (k f)", k=KD)
    up_v = w_up_e[0].rearrange("e (p k) f -> e p (k f)", k=KD)
    down_v = w_down_e[0].rearrange("e (c p) d -> e p c d", p=P)

    hn_dram = nc.dram_tensor("hn_rows", [S, D], F32, kind="Internal").ap()
    y_dram = nc.dram_tensor("y_rows", [(NQ - 1) * P, D], F32, kind="Internal").ap()
    y_blocks = y_dram.rearrange("(b s) d -> b s d", s=BLK)

    ctx = ExitStack()
    with ctx:
        def sb(name, shape, dt=F32):
            return ctx.enter_context(nc.sbuf_tensor(name, shape, dt))

        def sem(name):
            return ctx.enter_context(nc.semaphore(name))

        h = sb("h", [P, NT, D])
        ring = sb("ring", [P, 2, 3, 2048])
        work = sb("work", [P, 9984])
        front = sb("front", [P, 24576])
        slots = [ring[:, 0], ring[:, 1]] + [front[:, n * 6144:(n + 1) * 6144].rearrange("p (a b) -> p a b", a=3)
                                            for n in range(2)]
        xnT = front[:, 0:4096].rearrange("p (k t) -> p k t", k=KD)
        qTz = front[:, 0:4096].rearrange("p (h t) -> p h t", h=H)
        win = front[:, 4096:12288].rearrange("p (b k n) -> p b k n", b=2, k=KD)
        wout = front[:, 4096:12288].rearrange("p (k n) -> p k n", k=KD)
        proj = front[:, 12288:22528].rearrange("p (c t n) -> p c t n", c=5, t=NT)
        u_a, v_a, q_b, k_b, v_b = (proj[:, c] for c in range(5))
        ysq = front[:, 16384:18432].rearrange("p (j t) -> p j t", j=4)
        kT = front[:, 22528:24576].rearrange("p (j t) -> p j t", j=4)
        wple = front[:, 12288:14336].rearrange("p (k n) -> p k n", k=2)
        p_sb = front[:, 14336:15360].rearrange("p (t n) -> p t n", t=NT)
        pT = front[:, 15360:16384].rearrange("p (k t) -> p k t", k=2)
        hnT = front[:, 16384:20480].rearrange("p (k t) -> p k t", k=KD)
        zeros = front[:, 20480:21504]
        yT = work[:, 0:4096].rearrange("p (k t) -> p k t", k=8)
        pW = work[:, 0:4096].rearrange("p (t n) -> p t n", t=NT)
        probs = work[:, 4096:6144].rearrange("p (i k) -> p i k", i=NT)
        PT = work[:, 6144:8704].rearrange("p (b c q) -> p b c q", b=2, c=10)
        xs = work[:, 4096:6144].rearrange("p (b d) -> p b d", b=2)
        xg = xs
        junk = work[:, 6144:7168]
        xgT = work[:, 6144:8192].rearrange("p (b k s) -> p b k s", b=2, k=KD)
        sil = work[:, 8192:8448].rearrange("p (b f) -> p b f", b=2)
        act = work[:, 8448:8704].rearrange("p (b f) -> p b f", b=2)
        aT = work[:, 8704:8960].rearrange("p (b f) -> p b f", b=2)
        ysb = work[:, 8960:9984].rearrange("p (b n) -> p b n", b=2)
        wsb = work[:, 8192:8704].rearrange("p (g s) -> p g s", g=GA)
        sqs = work[:, 8704:9216]
        wsT = work[:, 9472:9984].rearrange("p (g t) -> p g t", g=GA)
        gva = sb("gva", [P, DA])
        hpT = front[:, 20480:22528].rearrange("p (b k t) -> p b k t", b=2, k=KD)
        sg = front[:, 22528:23552].rearrange("p (b n) -> p b n", b=2)
        wpg = front[:, 12288:20480].rearrange("p (k n) -> p k n", k=KD)
        yg = [slots[b].rearrange("p a b -> p (a b)")[:, 0:2 * D].rearrange("p (k d) -> p k d", k=2) for b in (0, 1)]

        ident = sb("ident", [P, P])
        causal = sb("causal", [P, P])
        earlier = sb("earlier", [P, P], BF16)
        ones_b = sb("ones_b", [P, P], BF16)
        ones1 = sb("ones1", [P, 1])
        g3 = sb("g3", [P, 3, KD])
        gqk = sb("gqk", [P, 2])
        goab = sb("goab", [P, 8])
        bs = sb("bs", [P, GA])
        wr = sb("wr", [P, KD, NG + E])
        ss3 = sb("ss3", [P, 3, NT])
        rs = sb("rs", [P, 3, NT])
        ssn = sb("ssn", [P, 3, 32])
        rsn = sb("rsn", [P, 3, 32])
        ssab = sb("ssab", [P, 2, NT])
        rsab = sb("rsab", [P, 2, NT])
        rt = sb("rt", [P, 32])
        mx = sb("mx", [P, H * NT])
        nmx = sb("nmx", [P, H * NT])
        rsum = sb("rsum", [P, H * NT])
        rrec = sb("rrec", [P, H * NT])
        scratch = front[:, 20480:24576]
        used = [0]

        def tmp(*shape, rows=P, dt=F32):
            n, at = 1, used[0]
            for d in shape:
                n *= d
            used[0] += n
            assert used[0] <= 4096
            v = scratch[0:rows, at:at + n]
            if dt is not F32:
                v = v.bitcast(dt)
            names = "abc"[:len(shape)]
            return v.rearrange(f"p ({' '.join(names)}) -> p {' '.join(names)}", **dict(zip(names, shape)))

        lgT = tmp(S, rows=NG + E)
        lg = tmp(NT, NG + E)
        r4 = tmp(NT, 4)
        oh_g = tmp(NT, NG)
        r32 = tmp(NT, E)
        s32 = tmp(NT, E)
        r8 = tmp(NT, EPG)
        t8 = tmp(NT, EPG)
        oh1 = tmp(NT, EPG)
        oh2 = tmp(NT, EPG)
        m12 = tmp(4, NT)
        M1 = tmp(NT, E)
        M2 = tmp(NT, E)
        cnt = tmp(E)
        incl = tmp(E)
        dlt = tmp(E)
        Ri = tmp(NT, E, dt=I32)
        Fi = tmp(NT, E, dt=I32)
        blkf = tmp(2, NT)
        modf = tmp(2, NT)
        slr = tmp(2, NT, dt=I32)
        slq = tmp(2, NT, dt=I32)
        slotf = tmp(2, NT)
        ohs = tmp(2, NT, P)
        ohb = tmp(2, NT, NQ)
        ovf = tmp(EXTRA + 2, E)
        ove = tmp(EXTRA + 2)
        nfl = tmp(1)
        Mb = sb("Mb", [P, NT, E], BF16)
        cw = sb("cw", [P, 2, NT])
        sloti = sb("sloti", [P, 2, NT], U32)
        idx = sb("idx", [P, NQ], U32)
        idxc = sb("idxc", [P, 2], U32)
        ovi = sb("ovi", [P, EXTRA + 2], I32)
        npi = sb("npi", [P, 1], I32)
        tokf = sb("tokf", [P, NT])
        ef = sb("ef", [P, E])
        first = sb("first", [P, EPG])
        slf = sb("slf", [P, P])
        zero = sb("zero", [P, 1])

        ps = [ctx.enter_context(nc.psum_tensor(f"ps{i}", [P, 512], F32)) for i in range(8)]

        ld_x = [sem(f"ld_x{t}") for t in range(NT)]
        ld_small = sem("ld_small")
        ld_win = [sem(f"ld_win{b}") for b in range(2)]
        ld_wout = [sem(f"ld_wout{b}") for b in range(2)]
        ld_ple = sem("ld_ple")
        ld_slot = [sem(f"ld_slot{b}") for b in range(RING)]
        ld_wpg = sem("ld_wpg")
        ld_xg = [sem(f"ld_xg{b}") for b in range(2)]
        ld_yg = [sem(f"ld_yg{b}") for b in range(2)]
        st_hn = [sem(f"st_hn{b}") for b in range(2)]
        st_y = [sem(f"st_y{b}") for b in range(2)]
        zeros_ready = sem("zeros_ready")
        st_zero = sem("st_zero")
        y_stored = sem("y_stored")
        st_out = sem("st_out")
        consts = sem("consts")
        sq_done = [sem(f"sq_done{k}") for k in range(3)]
        xs_ready = [sem(f"xs_ready{k}") for k in range(3)]
        xt_done = [sem(f"xt_done{k}") for k in range(3)]
        nT_ready = [sem(f"nT_ready{k}") for k in range(3)]
        ws_done = sem("ws_done")
        ws_ready = sem("ws_ready")
        proj_done = sem("proj_done")
        proj_ev = sem("proj_ev")
        qk_ready = sem("qk_ready")
        v_ready = sem("v_ready")
        qkt_done = sem("qkt_done")
        qkt_ready = sem("qkt_ready")
        qz_zero = sem("qz_zero")
        mix_done = sem("mix_done")
        ya_ready = sem("ya_ready")
        sa_done = sem("sa_done")
        ya_scaled = sem("ya_scaled")
        yat_done = sem("yat_done")
        yat_ready = sem("yat_ready")
        s_done = sem("s_done")
        nmx_ready = sem("nmx_ready")
        exp_done = sem("exp_done")
        p_ready = sem("p_ready")
        pt_done = sem("pt_done")
        pt_ready = sem("pt_ready")
        pv_done = sem("pv_done")
        yb_ready = sem("yb_ready")
        ysq_ready = sem("ysq_ready")
        sb_done = sem("sb_done")
        sb_read = sem("sb_read")
        wo_done = sem("wo_done")
        h_ready = sem("h_ready")
        lgt_done = sem("lgt_done")
        lgt_ready = sem("lgt_ready")
        lg_done = sem("lg_done")
        ex_in = sem("ex_in")
        ex_out = sem("ex_out")
        mb_ready = sem("mb_ready")
        rank_done = sem("rank_done")
        oh_ready = sem("oh_ready")
        idx_done = sem("idx_done")
        idx_ready = sem("idx_ready")
        col_ready = sem("col_ready")
        pp_done = sem("pp_done")
        pp_ready = sem("pp_ready")
        pw_done = sem("pw_done")
        pw_ready = sem("pw_ready")
        xgt_done = sem("xgt_done")
        xgt_ready = sem("xgt_ready")
        gu_done = sem("gu_done")
        sil_ready = sem("sil_ready")
        act_ready = sem("act_ready")
        at_done = sem("at_done")
        at_ready = sem("at_ready")
        block_done = sem("block_done")
        ysb_ready = sem("ysb_ready")
        h2_ready = sem("h2_ready")
        pg_done = sem("pg_done")
        sg_ready = sem("sg_ready")
        sg_used = sem("sg_used")
        out_ready = sem("out_ready")
        dve_step = sem("dve_step")
        pool_step = sem("pool_step")

        ORDER = [2, 3, 1, 4, 0]
        block = ctx.enter_context(nc.Block())

        @block.sync
        def _(sp):
            def load_expert(slot, gate, up, down):
                sp.dma_start(slots[slot][:, 0], gate).then_inc(ld_slot[slot], 16)
                sp.dma_start(slots[slot][:, 1], up).then_inc(ld_slot[slot], 16)
                sp.dma_start(slots[slot][:, 2].rearrange("p (c d) -> p c d", c=2), down).then_inc(ld_slot[slot], 16)

            def load_static(e):
                load_expert(e % RING, gate_v[e], up_v[e], down_v[e])

            def store_y(at, parity):
                for half in range(2):
                    sp.dma_start(at[:, half * 512:half * 512 + 512], ysb[64 * half:64 * half + 64, parity])\
                        .then_inc(st_y[parity], 16)

            for t in range(NT):
                sp.dma_start(h[:, t], x_v[t]).then_inc(ld_x[t], 16)
            for n in range(2):
                sp.dma_start(win[:, n], win_v[:, :, ORDER[n] * 512:ORDER[n] * 512 + 512]).then_inc(ld_win[n], 16)
            load_static(0)
            load_static(1)
            sp.wait_ge(zeros_ready, 1)
            for q in range(E // 2, NQ - 1):
                sp.dma_start(y_dram[q * P:q * P + P], zeros).then_inc(st_zero, 16)
            for n in range(2, 5):
                sp.wait_ge(proj_done, NT * (n - 1))
                sp.dma_start(win[:, n % 2], win_v[:, :, ORDER[n] * 512:ORDER[n] * 512 + 512])\
                    .then_inc(ld_win[n % 2], 16)
            for b, n in ((1, 3), (0, 4)):
                sp.wait_ge(proj_done, NT * (n + 1))
                sp.dma_start(wout[:, 4 * b:4 * b + 4], wout_v[:, 4 * b:4 * b + 4]).then_inc(ld_wout[b], 16)
            sp.wait_ge(yat_done, NT)
            sp.dma_start(wple, wple_v).then_inc(ld_ple, 16)
            sp.dma_start(p_sb, p_v).then_inc(ld_ple, 16)
            for t in range(NT):
                sp.wait_ge(xs_ready[1], t + 1)
                sp.dma_start(hn_dram[t * P:t * P + P], xs[:, t % 2]).then_inc(st_hn[t % 2], 16)
            sp.wait_ge(wo_done, 2 * NT)
            load_static(2)
            load_static(3)
            sp.wait_ge(pw_done, 2 * NT)
            sp.wait_ge(lgt_done, 1)
            sp.dma_start(wpg.rearrange("p k n -> p (k n)"), wpg_v).then_inc(ld_wpg, 16)
            with sp.Fori(0, (E - RING) // RING) as i:
                for s in range(RING):
                    e = RING * i + s
                    sp.wait_ge(block_done, e + 1)
                    load_expert(s, gate_v[bass.ds(e + RING, 1)].rearrange("a p n -> p (a n)"),
                                up_v[bass.ds(e + RING, 1)].rearrange("a p n -> p (a n)"),
                                down_v[bass.ds(e + RING, 1)].rearrange("a p c d -> p (a c) d"))
                    sp.wait_ge(ysb_ready, e + 1)
                    store_y(y_blocks[bass.ds(e, 1)].rearrange("a s d -> (a s) d"), s % 2)
            sp.wait_ge(idx_ready, 1)
            pairs = sp.value_load(npi[0:1, 0:1], min_val=1, max_val=EXTRA_PAIRS)
            for e in range(E - RING, E):
                sp.wait_ge(ysb_ready, e + 1)
                store_y(y_blocks[e], e % 2)
            with sp.Fori(0, pairs) as j:
                for s in range(2):
                    sp.wait_ge(block_done, 2 * j + (E + s - 1))
                    x_e = sp.value_load(ovi[0:1, bass.ds(2 * j + s, 1)], min_val=0, max_val=E - 1)
                    load_expert(s, gate_v[bass.ds(x_e, 1)].rearrange("a p n -> p (a n)"),
                                up_v[bass.ds(x_e, 1)].rearrange("a p n -> p (a n)"),
                                down_v[bass.ds(x_e, 1)].rearrange("a p c d -> p (a c) d"))
                for s in range(2):
                    sp.wait_ge(ysb_ready, 2 * j + (E + s + 1))
                    store_y(y_blocks[bass.ds(2 * j + (E + s), 1)].rearrange("a s d -> (a s) d"), s)
            sp.wait_ge(st_zero, 16 * (NQ - 1 - E // 2))
            for odd in range(2):
                sp.wait_ge(st_y[odd], 32 * pairs + 32 * (E // 2))
            sp.sem_inc(y_stored, 1)
            for t in range(NT):
                sp.wait_ge(out_ready, t + 1)
                sp.dma_start(out_v[t], h[:, t]).then_inc(st_out, 16)
            sp.wait_ge(st_out, 16 * NT)

        @block.gpsimd
        def _(pool):
            steps = [0]

            def link(ins):
                steps[0] += 1
                ins.then_inc(pool_step, 1)
                pool.wait_ge(pool_step, steps[0])

            small = [(g3[:, 0], g_mix[0].rearrange("(p k) -> p k", k=KD)),
                     (g3[:, 1], g_ffn[0].rearrange("(p k) -> p k", k=KD)),
                     (g3[:, 2], g_ple[0].rearrange("(p k) -> p k", k=KD)),
                     (gva[:, :], g_v_a[0:1, :].broadcast_to([P, DA])),
                     (wsb, w_s[0].rearrange("g t s -> t g s")),
                     (bs[:, :], b_s[0].rearrange("g t -> t g")),
                     (gqk[0:64, 0:1], g_q[0:1].rearrange("a d -> d a")),
                     (gqk[64:128, 0:1], g_q[0:1].rearrange("a d -> d a")),
                     (gqk[0:64, 1:2], g_k[0:1].rearrange("a d -> d a")),
                     (gqk[64:128, 1:2], g_k[0:1].rearrange("a d -> d a")),
                     (goab[:, 0:4], g_out_a[0].rearrange("(k p) -> p k", p=P)),
                     (goab[:, 4:8], g_out_b[0].rearrange("(k p) -> p k", p=P)),
                     (wr[:, :, 0:NG], w_group[0].rearrange("(p k) n -> p k n", k=KD)),
                     (wr[:, :, NG:], w_expert[0].rearrange("(p k) n -> p k n", k=KD))]
            assert len(small) == N_SMALL
            link(pool.memset(ident[:, :], 0.0))
            link(pool.affine_select(out=ident[:, :], in_=ident[:, :], compare_op=ALU.not_equal, fill=1.0, base=0,
                                    pattern=[[-1, P]], channel_multiplier=1))
            for dst, src in small:
                pool.dma_start(dst, src, allow_slow_non_contiguous=True).then_inc(ld_small, 16)
            link(pool.memset(causal[:, :], 0.0))
            pool.memset(zeros, 0.0).then_inc(zeros_ready, 1)
            pool.wait_ge(zeros_ready, 1)
            link(pool.affine_select(out=causal[:, :], in_=causal[:, :], compare_op=ALU.is_ge, fill=NEG, base=0,
                                    pattern=[[-1, P]], channel_multiplier=1))
            link(pool.memset(ones_b[:, :], 1.0))
            link(pool.affine_select(out=earlier[:, :], in_=ones_b[:, :], compare_op=ALU.is_gt, fill=0.0, base=0,
                                    pattern=[[1, P]], channel_multiplier=-1))
            link(pool.memset(ones1[:, :], 1.0))
            link(pool.memset(zero[:, :], 0.0))
            for dst, n, step, base, mult in ((tokf, NT, P, 0, 1), (ef, E, 1, 0, 0), (first, EPG, -1, EPG, 0),
                                             (slf, P, 1, 0, 0)):
                link(pool.iota(dst[:, :], pattern=[[step, n]], base=base, channel_multiplier=mult,
                               allow_small_or_imprecise_dtypes=True))
            pool.memset(zero[:, :], 0.0).then_inc(consts, 1)
            pool.wait_ge(ws_ready, 1)
            pool.affine_select(out=wsT, in_=wsT, compare_op=ALU.is_ge, fill=0.0, base=0,
                               pattern=[[0, GA], [1, P]], channel_multiplier=-1).then_inc(ws_ready, 1)
            pool.wait_ge(ws_ready, 2)
            pool.wait_ge(proj_done, 5 * NT)
            pool.memset(qTz[64:128].rearrange("p (j b) t -> p j b t", b=2)[:, :, 0], 0.0).then_inc(qz_zero, 1)
            pool.wait_ge(qz_zero, 1)
            pool.memset(qTz[0:64].rearrange("p (j b) t -> p j b t", b=2)[:, :, 1], 0.0).then_inc(qz_zero, 1)
            pool.wait_ge(idx_ready, 1)
            for b in range(2):
                pool.wait_ge(st_hn[b], 32)
            pairs = pool.value_load(npi[0:1, 0:1], min_val=1, max_val=EXTRA_PAIRS)

            def gather(col, parity):
                pool.indirect_dma_start(out=xg[:, parity], out_offset=None, in_=hn_dram,
                                        in_offset=bass.IndirectOffsetOnAxis(ap=col, axis=0))\
                    .then_inc(ld_xg[parity], 16)

            gather(idx[:, 0:1], 0)
            gather(idx[:, 1:2], 1)

            def gather_at(q, parity):
                pool.wait_ge(xgt_done, 2 * q - 2)
                pool.tensor_copy(idxc[:, parity:parity + 1], idx[:, bass.ds(q, 1)])
                pool.drain()
                gather(idxc[:, parity:parity + 1], parity)

            with pool.Fori(1, E // 4) as i:
                for s in range(2):
                    gather_at(2 * i + s, s)
            gather_at(E // 2, 0)
            with pool.Fori(0, pairs) as i:
                pool.wait_ge(xgt_done, 2 * i + (E + 2))
                pool.tensor_copy(idxc[:, 0:1], idx[:, bass.ds(i + (E // 2 + 1), 1)])
                pool.drain()
                gather(idxc[:, 0:1], 0)
            pool.wait_ge(y_stored, 1)
            for t in range(NT):
                if t >= 2:
                    pool.wait_ge(h2_ready, 2 * (t - 1))
                for k in range(2):
                    pool.indirect_dma_start(out=yg[t % 2][:, k], out_offset=None, in_=y_dram,
                                            in_offset=bass.IndirectOffsetOnAxis(ap=sloti[:, k, t:t + 1], axis=0))\
                        .then_inc(ld_yg[t % 2], 16)

        @block.tensor
        def _(pe):
            mm = nc.tensor.matmul

            def transposes_of_tile(k, t, banks):
                pe.wait_ge(xs_ready[k], t + 1)
                if t:
                    pe.wait_ge(nT_ready[k], t)
                rows = xs[:, t % 2].rearrange("p (a k) -> p k a", k=KD)
                for j in range(KD):
                    last = nc.tensor.transpose(ps[banks[j // 4]][:, j % 4 * P:j % 4 * P + P], rows[:, j], ident[:, :])
                last.then_inc(xt_done[k], 1)

            pe.wait_ge(consts, 1)
            pe.wait_ge(ld_small, 16 * N_SMALL)
            for g in range(GA):
                last = nc.tensor.transpose(ps[2][:, g * P:g * P + P], wsb[:, g], ident[:, :])
            last.then_inc(ws_done, 1)
            for t in range(NT):
                transposes_of_tile(0, t, (0, 1))
            for n in range(5):
                pe.wait_ge(ld_win[n % 2], 16 * (n // 2 + 1))
                for t in range(NT):
                    m = n * NT + t
                    if n == 0:
                        pe.wait_ge(nT_ready[0], t + 1)
                    if m >= 2:
                        pe.wait_ge(proj_ev, m - 1)
                    for k in range(KD):
                        last = mm(ps[4 + m % 2][:, :], xnT[:, k, t * P:t * P + P], win[:, n % 2, k],
                                  start=(k == 0), stop=(k == KD - 1))
                    last.then_inc(proj_done, 1)
            pe.wait_ge(qk_ready, 2 * NT)
            for t in range(NT):
                for w, src in enumerate((q_b, k_b)):
                    n = 2 * t + w
                    if n >= 2:
                        pe.wait_ge(qkt_ready, n - 1)
                    for j in range(4):
                        last = nc.tensor.transpose(ps[n % 2][:, j * P:j * P + P], src[:, t, j * P:j * P + P], ident[:, :])
                    last.then_inc(qkt_done, 1)
            pe.wait_ge(ws_ready, 2)
            pe.wait_ge(v_ready, NT)
            for g in range(GA):
                if g >= 2:
                    pe.wait_ge(ya_ready, g - 1)
                mm(ps[6 + g % 2][:, :], wsT[:, g], v_a[:, :, g * P:g * P + P], start=True, stop=True)\
                    .then_inc(mix_done, 1)

            def scores(hh, i):
                n = hh * NT + i
                if hh:
                    pe.wait_ge(exp_done, n - NT + 1)
                mm(ps[i][:, 0:(i + 1) * P], qTz[:, hh, i * P:i * P + P], kT[:, hh // 2, 0:(i + 1) * P],
                   start=True, stop=True).then_inc(s_done, 1)

            pe.wait_ge(qkt_ready, 2 * NT)
            pe.wait_ge(proj_ev, 5 * NT)
            for i in range(NT):
                scores(0, i)
            for hh in range(H):
                for i in range(NT):
                    n = hh * NT + i
                    if hh + 1 < H:
                        scores(hh + 1, i)
                    pe.wait_ge(p_ready, n + 1)
                    if n >= 2:
                        pe.wait_ge(pt_ready, n - 1)
                    for kt in range(i + 1):
                        last = nc.tensor.transpose(ps[4 + n % 2][:, kt * P:kt * P + P], probs[:, i, kt * P:kt * P + P],
                                                   ident[:, :])
                    last.then_inc(pt_done, 1)
                pe.wait_ge(pt_ready, NT * (hh + 1))
                if hh % 2 == 0:
                    if hh >= 4:
                        pe.wait_ge(yb_ready, hh // 2 - 1)
                        pe.wait_ge(ysq_ready, hh // 2 - 1)
                    else:
                        pe.wait_ge(ya_ready, GA)
                rows = slice(64 * (hh % 2), 64 * (hh % 2) + 64)
                for i in range(NT):
                    for kt in range(i + 1):
                        last = mm(ps[6 + hh // 2 % 2][rows, i * P:i * P + P], v_b[:, kt, hh * DH:hh * DH + DH],
                                  PT[:, hh % 2, i * (i + 1) // 2 + kt], start=(kt == 0), stop=(kt == i))
                last.then_inc(pv_done, 1)
            for t in range(NT):
                pe.wait_ge(ya_scaled, t + 1)
                if t >= 2:
                    pe.wait_ge(yat_ready, t - 1)
                elif t == 0:
                    pe.wait_ge(pt_ready, H * NT)
                for j in range(4):
                    last = nc.tensor.transpose(ps[4 + t % 2][:, j * P:j * P + P], u_a[:, t, j * P:j * P + P], ident[:, :])
                last.then_inc(yat_done, 1)
            pe.wait_ge(ysq_ready, 4)
            pe.wait_ge(yb_ready, 4)
            for t in range(NT):
                for j in range(4):
                    last = mm(ps[6][:, t:t + 1], ysq[:, j, t * P:t * P + P], ones1[:, :], start=(j == 0), stop=(j == 3))
            last.then_inc(sb_done, 1)
            pe.wait_ge(ld_wout[0], 16)
            pe.wait_ge(ld_wout[1], 16)
            pe.wait_ge(yat_ready, NT)

            def output_rows(t):
                for half in range(2):
                    n = 2 * t + half
                    if n >= 2:
                        pe.wait_ge(h_ready, n - 1)
                    for w in range(2):
                        for k in range(4):
                            last = mm(ps[2 * (n % 2) + w][:, :], yT[:, 4 * w + k, t * P:t * P + P],
                                      wout[:, 4 * w + k, half * 512:half * 512 + 512], start=(k == 0), stop=(k == 3))
                    last.then_inc(wo_done, 1)

            for t in range(NT):
                output_rows(t)
                if t:
                    transposes_of_tile(1, t - 1, (4, 5))
            pe.wait_ge(ld_ple, 32)

            def embedding(t):
                pe.wait_ge(pp_ready, t + 1)
                for half in range(2):
                    n = 2 * t + half
                    if n >= 2:
                        pe.wait_ge(pw_ready, n - 1)
                    for k in range(2):
                        last = mm(ps[n % 2][:, :], pT[:, k, t * P:t * P + P], wple[:, k, half * 512:half * 512 + 512],
                                  start=(k == 0), stop=(k == 1))
                    last.then_inc(pw_done, 1)

            for t in range(NT):
                if t:
                    pe.wait_ge(pp_ready, t)
                for k in range(2):
                    last = nc.tensor.transpose(ps[7][:, k * P:k * P + P], p_sb[:, t, k * P:k * P + P], ident[:, :])
                last.then_inc(pp_done, 1)
            transposes_of_tile(1, NT - 1, (4, 5))
            pe.wait_ge(nT_ready[1], NT)
            pe.wait_ge(sb_read, 1)
            for k in range(KD):
                last = mm(ps[6][0:NG + E, :], wr[:, k], hnT[:, k], start=(k == 0), stop=(k == KD - 1))
            last.then_inc(lgt_done, 1)
            pe.wait_ge(lgt_ready, 1)
            for t in range(NT):
                last = nc.tensor.transpose(ps[4][:, t * (NG + E):(t + 1) * (NG + E)], lgT[:, t * P:t * P + P],
                                           ident[0:NG + E, 0:NG + E])
            last.then_inc(lg_done, 1)
            pe.wait_ge(h_ready, 2 * NT)
            embedding(0)
            pe.wait_ge(mb_ready, 1)
            for t in range(NT):
                for t2 in range(t + 1):
                    mm(ps[5][:, t * E:t * E + E], (earlier if t2 == t else ones_b)[:, :], Mb[:, t2],
                       start=(t2 == 0), stop=(t2 == t))
            for t2 in range(NT):
                last = mm(ps[5][:, NT * E:NT * E + E], ones_b[:, :], Mb[:, t2], start=(t2 == 0), stop=(t2 == NT - 1))
            last.then_inc(rank_done, 1)
            embedding(1)
            pe.wait_ge(oh_ready, 1)
            for n in range(2 * NT):
                last = mm(ps[6][:, 0:NQ], ohs[:, n // NT, n % NT], ohb[:, n // NT, n % NT],
                          start=(n == 0), stop=(n == 2 * NT - 1))
            last.then_inc(idx_done, 1)
            embedding(2)
            embedding(3)
            pe.wait_ge(idx_ready, 1)
            pairs = pe.value_load(npi[0:1, 0:1], min_val=1, max_val=EXTRA_PAIRS)

            def transpose_half(parity, half, gathered):
                pe.wait_ge(ld_xg[parity], gathered)
                rows = xg[:, parity].rearrange("p (a k) -> p k a", k=KD)
                for k in range(4):
                    last = nc.tensor.transpose(ps[6 + half][:, k * P:k * P + P], rows[:, 4 * half + k], ident[:, :])
                last.then_inc(xgt_done, 1)

            def expert_block(b, odd, slot, parity, loaded, ahead, fresh=False):
                w = slots[slot]
                pe.wait_ge(xgt_ready, b + (2 - odd))
                pe.wait_ge(ld_slot[slot], loaded)
                if not fresh:
                    pe.wait_ge(act_ready, b - 1)
                for k in range(KD):
                    for c in range(2):
                        last = mm(ps[odd][64 * c:64 * c + 64, 0:256], xgT[:, parity, k, odd * BLK:odd * BLK + BLK],
                                  w[:, 0:2, k * FF + c * P:k * FF + c * P + P], start=(k == 0), stop=(k == KD - 1))
                last.then_inc(gu_done, 1)
                for to, half, gathered in ahead:
                    transpose_half(to, half, gathered)
                pe.wait_ge(act_ready, b + 1)
                nc.tensor.transpose(ps[4][:, odd * P:odd * P + P], act[:, odd], ident[:, :]).then_inc(at_done, 1)
                pe.wait_ge(at_ready, b + 1)
                if not fresh:
                    pe.wait_ge(ysb_ready, b - 1)
                for c in range(2):
                    for half in range(2):
                        last = mm(ps[2 + odd][64 * half:64 * half + 64, :], aT[:, odd, c * 64:c * 64 + 64],
                                  w[:, 2, c * D + half * 512:c * D + half * 512 + 512], start=(c == 0), stop=(c == 1))
                last.then_inc(block_done, 1)

            pe.wait_ge(pw_ready, 2 * NT)
            transpose_half(0, 0, 16)
            transpose_half(0, 1, 16)
            for b in range(RING):
                q = b // 2 + 1
                expert_block(b, b % 2, b, b // 2 % 2, 48, [(q % 2, b % 2, 16 * (q // 2 + 1))], fresh=b < 2)
            with pe.Fori(1, E // RING) as i:
                for s in range(RING):
                    q = s // 2 + 1
                    expert_block(RING * i + s, s % 2, s, s // 2, 48 * i + 48,
                                 [(q % 2, s % 2, 16 * i + 16 * (q // 2 + 1))])
            with pe.Fori(0, pairs) as j:
                for s in range(2):
                    ahead = [(0, half, 16 * j + 16 * (E // 4 + 2)) for half in range(2)] if s else []
                    expert_block(2 * j + (E + s), s, s, 0, 48 * j + 48 * (E // RING + 1), ahead)
            pe.wait_ge(ld_wpg, 16)
            for t in range(NT):
                transposes_of_tile(2, t, (4, 5))
                for half in range(2):
                    n = 2 * t + half
                    if half == 0:
                        pe.wait_ge(nT_ready[2], t + 1)
                    if n >= 2:
                        pe.wait_ge(sg_ready, n - 1)
                    else:
                        pe.wait_ge(act_ready, 2 * pairs + E)
                    for k in range(KD):
                        last = mm(ps[n % 2][:, :], hpT[:, t % 2, k], wpg[:, k, half * 512:half * 512 + 512],
                                  start=(k == 0), stop=(k == KD - 1))
                    last.then_inc(pg_done, 1)

        @block.scalar
        def _(act_e):
            e_ = nc.scalar

            def squares(k, t):
                e_.activation(junk, h[:, t], ACT.Square, accum_out=ss3[:, k, t:t + 1]).then_inc(sq_done[k], 1)
                act_e.wait_ge(sq_done[k], t + 1)

            for t in range(NT):
                act_e.wait_ge(ld_x[t], 16)
                squares(0, t)
            for n, c in enumerate(ORDER):
                if c == 4:
                    act_e.wait_ge(st_zero, 16 * (NQ - 1 - E // 2))
                for t in range(NT):
                    m = n * NT + t
                    act_e.wait_ge(proj_done, m + 1)
                    e_.activation(proj[:, c, t], ps[4 + m % 2][:, :], ACT.Gelu_apprx_tanh if c < 2 else ACT.Copy)\
                        .then_inc(proj_ev, 1)
            act_e.wait_ge(ya_ready, GA)
            for t in range(NT):
                e_.activation(junk[:, 0:DA], u_a[:, t], ACT.Square, accum_out=ssab[:, 0, t:t + 1]).then_inc(sa_done, 1)
                act_e.wait_ge(sa_done, t + 1)

            def exps(hh, i):
                n = hh * NT + i
                act_e.wait_ge(nmx_ready, n + 1)
                e_.activation(probs[:, i, 0:(i + 1) * P], ps[i][:, 0:(i + 1) * P], ACT.Exp, bias=nmx[:, n:n + 1],
                              scale=DH ** -0.5, accum_out=rsum[:, n:n + 1]).then_inc(exp_done, 1)

            for i in range(NT):
                exps(0, i)
            for hh in range(H):
                for i in range(NT):
                    n = hh * NT + i
                    act_e.wait_ge(pt_done, n + 1)
                    if hh >= 2:
                        act_e.wait_ge(pv_done, hh - 1)
                    e_.activation(PT[:, hh % 2, i * (i + 1) // 2:(i + 1) * (i + 2) // 2].rearrange("p a b -> p (a b)"),
                                  ps[4 + n % 2][:, 0:(i + 1) * P], ACT.Copy).then_inc(pt_ready, 1)
                    if hh + 1 < H:
                        exps(hh + 1, i)
                if hh % 2:
                    j = hh // 2
                    act_e.wait_ge(yb_ready, j + 1)
                    e_.activation(ysq[:, j], ps[6 + j % 2][:, :], ACT.Square).then_inc(ysq_ready, 1)
            for t in range(NT):
                act_e.wait_ge(h_ready, 2 * (t + 1))
                if t == 0:
                    act_e.wait_ge(pv_done, H)
                squares(1, t)
            for t in range(NT):
                act_e.wait_ge(pp_done, t + 1)
                e_.activation(pT[:, :, t * P:t * P + P], ps[7][:, 0:2 * P].rearrange("p (k t) -> p k t", k=2), ACT.Copy)\
                    .then_inc(pp_ready, 1)
            act_e.wait_ge(lgt_done, 1)
            e_.activation(lgT[:, :], ps[6][0:NG + E, :], ACT.Copy).then_inc(lgt_ready, 1)
            act_e.wait_ge(ex_in, 1)
            e_.activation(lg[:, :, 0:NG], lg[:, :, 0:NG], ACT.Exp).then_inc(ex_out, 1)
            act_e.wait_ge(ex_in, 2)
            e_.activation(m12[:, 2], m12[:, 1], ACT.Exp).then_inc(ex_out, 1)
            for n in range(2 * NT):
                act_e.wait_ge(pw_done, n + 1)
                e_.activation(pW[:, n // 2, n % 2 * 512:n % 2 * 512 + 512], ps[n % 2][:, :], ACT.Copy)\
                    .then_inc(pw_ready, 1)
            act_e.wait_ge(idx_ready, 1)
            pairs = act_e.value_load(npi[0:1, 0:1], min_val=1, max_val=EXTRA_PAIRS)

            def block_act(b, parity, stored=None):
                act_e.wait_ge(gu_done, b + 1)
                if stored is not None:
                    act_e.wait_ge(act_ready, b - 1)
                e_.activation(sil[:, parity], ps[parity][:, 0:P], ACT.Silu).then_inc(sil_ready, 1)
                act_e.wait_ge(block_done, b + 1)
                if stored is not None:
                    act_e.wait_ge(st_y[parity], stored)
                e_.activation(ysb[:, parity], ps[2 + parity][:, :], ACT.Copy).then_inc(ysb_ready, 1)

            for b in range(2):
                block_act(b, b)
            with act_e.Fori(0, (E - 2) // 2) as i:
                for s in range(2):
                    block_act(2 * i + (2 + s), s, 32 * i + 32)
            with act_e.Fori(0, pairs) as j:
                for s in range(2):
                    block_act(2 * j + (E + s), s, 32 * j + 32 * (E // 2))

            def sigmoids(t):
                for half in range(2):
                    n = 2 * t + half
                    act_e.wait_ge(pg_done, n + 1)
                    if n >= 2:
                        act_e.wait_ge(sg_used, n - 1)
                    e_.activation(sg[:, n % 2], ps[n % 2][:, :], ACT.Sigmoid).then_inc(sg_ready, 1)

            for t in range(NT):
                act_e.wait_ge(h2_ready, 2 * (t + 1))
                squares(2, t)
                if t:
                    sigmoids(t - 1)
            sigmoids(NT - 1)

        @block.vector
        def _(dve):
            v = nc.vector
            steps = [0]

            def link(ins):
                steps[0] += 1
                ins.then_inc(dve_step, 1)
                dve.wait_ge(dve_step, steps[0])

            def rsqrt(dst, m, n, width):
                t = rt[:, 0:width]
                link(v.tensor_scalar(m, m, 1.0 / n, EPS, ALU.mult, ALU.add))
                link(v.tensor_scalar(dst.bitcast(I32), m.bitcast(I32), 1, None, ALU.logical_shift_right))
                link(v.tensor_scalar(dst.bitcast(I32), dst.bitcast(I32), -1.0, MAGIC, ALU.mult, ALU.add))
                for _ in range(3):
                    link(v.tensor_tensor(t, dst, dst, ALU.mult))
                    link(v.scalar_tensor_tensor(out=t, in0=t, scalar=-0.5, in1=m, op0=ALU.mult, op1=ALU.mult))
                    link(v.scalar_tensor_tensor(out=dst, in0=t, scalar=1.5, in1=dst, op0=ALU.add, op1=ALU.mult))

            def scaled_rows(k, t):
                dve.wait_ge(sq_done[k], t + 1)
                rsqrt(rs[:, k, t:t + 1], ss3[:, k, t:t + 1], D, 1)
                if t >= 2:
                    dve.wait_ge(xt_done[k], t - 1)
                    if k == 1:
                        dve.wait_ge(st_hn[t % 2], 16)
                v.tensor_scalar(xs[:, t % 2], h[:, t], rs[:, k, t:t + 1], None, ALU.mult).then_inc(xs_ready[k], 1)

            def normed(k, t, dst, banks):
                dve.wait_ge(xt_done[k], t + 1)
                for b in range(2):
                    ins = v.tensor_tensor(dst[:, 4 * b:4 * b + 4],
                                          ps[banks[b]][:, :].rearrange("p (k t) -> p k t", k=4),
                                          g3[:, k, 4 * b:4 * b + 4].unsqueeze(2).broadcast_to([P, 4, P]), ALU.mult)
                ins.then_inc(nT_ready[k], 1)

            dve.wait_ge(ld_small, 16 * N_SMALL)
            dve.wait_ge(ws_done, 1)
            v.tensor_copy(wsT.rearrange("p g t -> p (g t)"), ps[2][:, :]).then_inc(ws_ready, 1)
            for t in range(NT):
                scaled_rows(0, t)
                normed(0, t, xnT[:, :, t * P:t * P + P], (0, 1))
            for n, c in enumerate(ORDER[0:3]):
                w = DH if n < 2 else P
                m = DA // w
                for t in range(NT):
                    dve.wait_ge(proj_ev, n * NT + t + 1)
                    link(v.tensor_tensor(sqs, proj[:, c, t], proj[:, c, t], ALU.mult))
                    link(v.tensor_reduce(ssn[:, n, t * m:t * m + m], sqs.rearrange("p (a b) -> p a b", b=w),
                                         axis=AX.X, op=ALU.add))
                rsqrt(rsn[:, n, 0:NT * m], ssn[:, n, 0:NT * m], w, NT * m)
                for t in range(NT):
                    a = proj[:, c, t].rearrange("p (a b) -> p a b", b=w)
                    ins = v.tensor_tensor(a, a, rsn[:, n, t * m:t * m + m].unsqueeze(2).broadcast_to([P, m, w]), ALU.mult)
                    if n < 2:
                        ins.then_inc(qk_ready, 1)
                    else:
                        link(ins)
                        v.tensor_tensor(v_a[:, t], v_a[:, t], gva[:, :], ALU.mult).then_inc(v_ready, 1)
            dve.wait_ge(qz_zero, 2)
            for t in range(NT):
                dve.wait_ge(qkt_done, 2 * t + 1)
                src = ps[0][:, :].rearrange("p (j t) -> p j t", j=4)
                for b in range(2):
                    rows = slice(64 * b, 64 * b + 64)
                    ins = v.tensor_scalar(qTz[rows].rearrange("p (j b) t -> p j b t", b=2)[:, :, b, t * P:t * P + P],
                                          src[rows], gqk[rows, 0:1], None, ALU.mult)
                ins.then_inc(qkt_ready, 1)
                dve.wait_ge(qkt_done, 2 * t + 2)
                v.tensor_scalar(kT[:, :, t * P:t * P + P], ps[1][:, :].rearrange("p (j t) -> p j t", j=4),
                                gqk[:, 1:2], None, ALU.mult).then_inc(qkt_ready, 1)
            dve.wait_ge(proj_ev, 5 * NT)
            for g in range(GA):
                dve.wait_ge(mix_done, g + 1)
                u = u_a[:, :, g * P:g * P + P]
                v.scalar_tensor_tensor(out=u, in0=ps[6 + g % 2][:, :].rearrange("p (n d) -> p n d", n=NT),
                                       scalar=bs[:, g:g + 1], in1=u, op0=ALU.add, op1=ALU.mult).then_inc(ya_ready, 1)

            def row_max(hh, i):
                n = hh * NT + i
                dve.wait_ge(s_done, n + 1)
                diag = ps[i][:, i * P:i * P + P]
                link(v.tensor_tensor(diag, diag, causal[:, :], ALU.add))
                link(v.tensor_reduce(mx[:, n:n + 1], ps[i][:, 0:(i + 1) * P], axis=AX.X, op=ALU.max))
                v.tensor_scalar(nmx[:, n:n + 1], mx[:, n:n + 1], -DH ** -0.5, None, ALU.mult).then_inc(nmx_ready, 1)

            for i in range(NT):
                row_max(0, i)
            dve.wait_ge(sa_done, NT)
            rsqrt(rsab[:, 0], ssab[:, 0], DA, NT)
            for t in range(NT):
                v.tensor_scalar(u_a[:, t], u_a[:, t], rsab[:, 0, t:t + 1], None, ALU.mult).then_inc(ya_scaled, 1)
            for hh in range(H):
                for i in range(NT):
                    n = hh * NT + i
                    dve.wait_ge(exp_done, n + 1)
                    link(v.reciprocal(rrec[:, n:n + 1], rsum[:, n:n + 1]))
                    v.tensor_scalar(probs[:, i, 0:(i + 1) * P], probs[:, i, 0:(i + 1) * P], rrec[:, n:n + 1], None,
                                    ALU.mult).then_inc(p_ready, 1)
                    if hh + 1 < H:
                        row_max(hh + 1, i)
                if hh % 2:
                    j = hh // 2
                    dve.wait_ge(pv_done, hh + 1)
                    v.tensor_scalar(yT[:, 4 + j], ps[6 + j % 2][:, :], goab[:, 4 + j:5 + j], None, ALU.mult)\
                        .then_inc(yb_ready, 1)
            for t in range(NT):
                dve.wait_ge(yat_done, t + 1)
                v.tensor_tensor(yT[:, 0:4, t * P:t * P + P], ps[4 + t % 2][:, :].rearrange("p (k t) -> p k t", k=4),
                                goab[:, 0:4].unsqueeze(2).broadcast_to([P, 4, P]), ALU.mult).then_inc(yat_ready, 1)
            dve.wait_ge(sb_done, 1)
            v.tensor_copy(ssab[:, 1], ps[6][:, 0:NT]).then_inc(sb_read, 1)
            dve.wait_ge(sb_read, 1)
            rsqrt(rsab[:, 1], ssab[:, 1], DA, NT)
            for t in range(NT):
                for half in range(2):
                    n = 2 * t + half
                    dve.wait_ge(wo_done, n + 1)
                    cols = h[:, t, half * 512:half * 512 + 512]
                    link(v.tensor_tensor(cols, cols, ps[2 * (n % 2)][:, :], ALU.add))
                    v.scalar_tensor_tensor(out=cols, in0=ps[2 * (n % 2) + 1][:, :], scalar=rsab[:, 1, t:t + 1], in1=cols,
                                           op0=ALU.mult, op1=ALU.add).then_inc(h_ready, 1)
                scaled_rows(1, t)
                if t:
                    normed(1, t - 1, hnT[:, :, (t - 1) * P:t * P], (4, 5))
            normed(1, NT - 1, hnT[:, :, (NT - 1) * P:NT * P], (4, 5))
            dve.wait_ge(lg_done, 1)
            link(v.tensor_copy(lg[:, :, :], ps[4][:, 0:NT * (NG + E)].rearrange("p (t n) -> p t n", t=NT)))

            def col(a):
                return a.unsqueeze(2)

            def one_hot_of_max(dst, src, top, n):
                link(v.tensor_reduce(top, src, axis=AX.X, op=ALU.max))
                link(v.tensor_tensor(dst, src, col(top).broadcast_to([P, NT, n]), ALU.is_equal))
                link(v.tensor_tensor(dst, dst, first[:, 0:n].unsqueeze(1).broadcast_to([P, NT, n]), ALU.mult))
                link(v.tensor_reduce(r4[:, :, 3], dst, axis=AX.X, op=ALU.max))
                link(v.tensor_tensor(dst, dst, col(r4[:, :, 3]).broadcast_to([P, NT, n]), ALU.is_equal))

            one_hot_of_max(oh_g[:, :, :], lg[:, :, 0:NG], r4[:, :, 0], NG)
            v.tensor_tensor(lg[:, :, 0:NG], lg[:, :, 0:NG], col(r4[:, :, 0]).broadcast_to([P, NT, NG]), ALU.subtract)\
                .then_inc(ex_in, 1)
            oh_gb = oh_g[:, :, :].unsqueeze(3).broadcast_to([P, NT, NG, EPG])
            l4 = s32[:, :, :].rearrange("p t (g e) -> p t g e", g=NG)
            for t in range(NT):
                link(v.tensor_tensor(l4[:, t], lg[:, t, NG:].rearrange("p (g e) -> p g e", g=NG), oh_gb[:, t], ALU.mult))
            link(v.tensor_reduce(r8[:, :, :], s32[:, :, :].rearrange("p t (g e) -> p t e g", g=NG), axis=AX.X, op=ALU.add))
            one_hot_of_max(oh1[:, :, :], r8[:, :, :], m12[:, 0], EPG)
            link(v.scalar_tensor_tensor(out=t8[:, :, :], in0=oh1[:, :, :], scalar=-BIG, in1=r8[:, :, :],
                                        op0=ALU.mult, op1=ALU.add))
            one_hot_of_max(oh2[:, :, :], t8[:, :, :], m12[:, 1], EPG)
            v.tensor_tensor(m12[:, 1], m12[:, 1], m12[:, 0], ALU.subtract).then_inc(ex_in, 1)
            for t in range(NT):
                for M, oh in ((M1, oh1), (M2, oh2)):
                    link(v.tensor_tensor(M[:, t].rearrange("p (g e) -> p g e", g=NG), oh_gb[:, t],
                                         oh[:, t:t + 1].broadcast_to([P, NG, EPG]), ALU.mult))
            v.tensor_tensor(Mb[:, :, :], M1[:, :, :], M2[:, :, :], ALU.add).then_inc(mb_ready, 1)
            dve.wait_ge(ex_out, 2)
            link(v.tensor_reduce(r4[:, :, 1], lg[:, :, 0:NG], axis=AX.X, op=ALU.add))
            link(v.tensor_scalar(m12[:, 3], m12[:, 2], 1.0, None, ALU.add))
            link(v.tensor_tensor(r4[:, :, 1], r4[:, :, 1], m12[:, 3], ALU.mult))
            link(v.reciprocal(cw[:, 0], r4[:, :, 1]))
            link(v.tensor_tensor(cw[:, 1], cw[:, 0], m12[:, 2], ALU.mult))
            dve.wait_ge(rank_done, 1)
            link(v.tensor_copy(r32[:, :, :], ps[5][:, 0:NT * E].rearrange("p (t e) -> p t e", t=NT)))
            link(v.tensor_copy(s32[:, 0], ps[5][:, NT * E:NT * E + E]))
            link(v.tensor_scalar(cnt[:, :], s32[:, 0], float(BLK), None, ALU.is_gt))
            for n in range(2, S // BLK):
                link(v.scalar_tensor_tensor(out=cnt[:, :], in0=s32[:, 0], scalar=float(n * BLK), in1=cnt[:, :],
                                            op0=ALU.is_gt, op1=ALU.add))
            link(v.tensor_tensor_scan(out=incl[:, :], data0=cnt[:, :], data1=cnt[:, :], initial=0.0,
                                      op0=ALU.add, op1=ALU.max))
            link(v.tensor_scalar(ovf[:, 0, 0:EXTRA_PAIRS], slf[:, 0:EXTRA_PAIRS], 2.0, None, ALU.mult))
            link(v.tensor_scalar(ovf[:, 0, 0:EXTRA_PAIRS], ovf[:, 0, 0:EXTRA_PAIRS], incl[:, E - 1:E], None,
                                 ALU.is_lt))
            link(v.tensor_reduce(nfl[:, :], ovf[:, 0, 0:EXTRA_PAIRS], axis=AX.X, op=ALU.add))
            link(v.tensor_scalar(nfl[:, :], nfl[:, :], 1.0, None, ALU.max))
            link(v.tensor_copy(npi[:, :], nfl[:, :]))
            link(v.tensor_tensor(ovf[:, :, :], incl[:, :].unsqueeze(1).broadcast_to([P, EXTRA + 2, E]),
                                 slf[:, 0:EXTRA + 2].unsqueeze(2).broadcast_to([P, EXTRA + 2, E]), ALU.is_le))
            link(v.tensor_reduce(ove[:, :], ovf[:, :, :], axis=AX.X, op=ALU.add))
            link(v.tensor_scalar(ove[:, :], ove[:, :], float(E - 1), None, ALU.min))
            link(v.tensor_copy(ovi[:, :], ove[:, :]))
            link(v.tensor_tensor(dlt[:, :], incl[:, :], cnt[:, :], ALU.subtract))
            link(v.scalar_tensor_tensor(out=dlt[:, :], in0=dlt[:, :], scalar=float(E - 1), in1=ef[:, :],
                                        op0=ALU.add, op1=ALU.subtract))
            link(v.tensor_copy(Ri[:, :, :], r32[:, :, :]))
            link(v.tensor_scalar(Fi[:, :, :], Ri[:, :, :], 6, None, ALU.logical_shift_right))
            link(v.tensor_scalar(Ri[:, :, :], Ri[:, :, :], BLK - 1, None, ALU.bitwise_and))
            link(v.tensor_copy(s32[:, :, :], Fi[:, :, :]))
            link(v.tensor_scalar(r32[:, :, :], s32[:, :, :], 1.0, None, ALU.min))
            link(v.tensor_tensor(r32[:, :, :], r32[:, :, :], dlt[:, :].unsqueeze(1).broadcast_to([P, NT, E]), ALU.mult))
            link(v.tensor_tensor(r32[:, :, :], r32[:, :, :], s32[:, :, :], ALU.add))
            link(v.tensor_tensor(r32[:, :, :], r32[:, :, :], ef[:, :].unsqueeze(1).broadcast_to([P, NT, E]), ALU.add))
            for k, M in ((0, M1), (1, M2)):
                link(v.tensor_tensor(s32[:, :, :], M[:, :, :], r32[:, :, :], ALU.mult))
                link(v.tensor_reduce(blkf[:, k], s32[:, :, :], axis=AX.X, op=ALU.add))
                link(v.tensor_tensor(s32[:, :, :], M[:, :, :], Ri[:, :, :], ALU.mult))
                link(v.tensor_reduce(modf[:, k], s32[:, :, :], axis=AX.X, op=ALU.add))
            link(v.scalar_tensor_tensor(out=slotf[:, :, :], in0=blkf[:, :, :], scalar=float(BLK), in1=modf[:, :, :],
                                        op0=ALU.mult, op1=ALU.add))
            link(v.tensor_copy(sloti[:, :, :], slotf[:, :, :]))
            link(v.tensor_copy(slr[:, :, :], slotf[:, :, :]))
            link(v.tensor_scalar(slq[:, :, :], slr[:, :, :], 7, None, ALU.logical_shift_right))
            link(v.tensor_scalar(slr[:, :, :], slr[:, :, :], P - 1, None, ALU.bitwise_and))
            link(v.tensor_copy(blkf[:, :, :], slq[:, :, :]))
            link(v.tensor_copy(modf[:, :, :], slr[:, :, :]))
            for k in range(2):
                for t in range(NT):
                    link(v.tensor_scalar(ohs[:, k, t], slf[:, :], modf[:, k, t:t + 1], None, ALU.is_equal))
                    last = v.tensor_scalar(ohb[:, k, t], slf[:, 0:NQ], blkf[:, k, t:t + 1], tokf[:, t:t + 1],
                                           ALU.is_equal, ALU.mult)
                    if (k, t) != (1, NT - 1):
                        link(last)
            last.then_inc(oh_ready, 1)
            dve.wait_ge(idx_done, 1)
            v.tensor_copy(idx[:, :], ps[6][:, 0:NQ]).then_inc(idx_ready, 1)
            dve.wait_ge(idx_ready, 1)
            pairs = dve.value_load(npi[0:1, 0:1], min_val=1, max_val=EXTRA_PAIRS)

            def xgt_copy(m, parity, half):
                dve.wait_ge(xgt_done, m + 1)
                v.tensor_tensor(xgT[:, parity, 4 * half:4 * half + 4],
                                ps[6 + half][:, :].rearrange("p (k s) -> p k s", k=4),
                                g3[:, 1, 4 * half:4 * half + 4].unsqueeze(2).broadcast_to([P, 4, P]), ALU.mult)\
                    .then_inc(xgt_ready, 1)

            def block_dve(b, odd, ahead, fresh=False):
                dve.wait_ge(sil_ready, b + 1)
                if not fresh:
                    dve.wait_ge(at_done, b - 1)
                v.tensor_tensor(act[:, odd], sil[:, odd], ps[odd][:, P:2 * P], ALU.mult).then_inc(act_ready, 1)
                for m, parity, half in ahead:
                    xgt_copy(m, parity, half)
                dve.wait_ge(at_done, b + 1)
                if not fresh:
                    dve.wait_ge(block_done, b - 1)
                v.tensor_copy(aT[:, odd], ps[4][:, odd * P:odd * P + P]).then_inc(at_ready, 1)

            xgt_copy(0, 0, 0)
            xgt_copy(1, 0, 1)
            for b in range(RING):
                block_dve(b, b % 2, [(b + 2, (b // 2 + 1) % 2, b % 2)], fresh=b < 2)
            with dve.Fori(1, E // RING) as i:
                for s in range(RING):
                    b = RING * i + s
                    block_dve(b, s % 2, [(RING * i + (s + 2), (s // 2 + 1) % 2, s % 2)])
            with dve.Fori(0, pairs) as j:
                block_dve(2 * j + E, 0, [])
                block_dve(2 * j + (E + 1), 1, [(2 * j + (E + 2), 0, 0), (2 * j + (E + 3), 0, 1)])
            def combine(t):
                dve.wait_ge(ld_yg[t % 2], 32 * (t // 2 + 1))
                for k in range(2):
                    v.scalar_tensor_tensor(out=h[:, t], in0=yg[t % 2][:, k], scalar=cw[:, k, t:t + 1], in1=h[:, t],
                                           op0=ALU.mult, op1=ALU.add).then_inc(h2_ready, 1)
                    dve.wait_ge(h2_ready, 2 * t + k + 1)

            def finish(t):
                for half in range(2):
                    n = 2 * t + half
                    dve.wait_ge(sg_ready, n + 1)
                    c = slice(half * 512, half * 512 + 512)
                    v.tensor_tensor(pW[:, t, c], pW[:, t, c], sg[:, n % 2], ALU.mult).then_inc(sg_used, 1)
                    dve.wait_ge(sg_used, n + 1)
                    last = v.tensor_tensor(h[:, t, c], h[:, t, c], pW[:, t, c], ALU.add)
                    if half == 0:
                        link(last)
                last.then_inc(out_ready, 1)

            for t in range(NT):
                combine(t)
                scaled_rows(2, t)
                if t:
                    finish(t - 1)
                normed(2, t, hpT[:, t % 2], (4, 5))
            finish(NT - 1)


_INS = ["x", "p", "g_mix", "w_in", "g_v_a", "w_s", "b_s", "g_q", "g_k", "g_out_a", "g_out_b", "w_out", "g_ffn",
        "w_group", "w_expert", "w_gate_e", "w_up_e", "w_down_e", "g_ple", "w_ple", "w_ple_gate"]


def kernel(**inputs):
    import numpy as np
    import concourse.bacc as bacc
    from concourse.bass_utils import run_bass_kernel_spmd

    nc = bacc.Bacc("TRN2", target_bir_lowering=False, num_devices=1)
    arrays, args = {}, []
    for name in _INS:
        a = np.ascontiguousarray(inputs[name])
        arrays[f"in_{name}"] = a
        args.append(nc.dram_tensor(f"in_{name}", a.shape, mybir.dt.from_np(a.dtype), kind="ExternalInput").ap())
    out = nc.dram_tensor("out_h", (1, S, D), F32, kind="ExternalOutput").ap()
    hybrid_layer(nc, *args, out)
    r = run_bass_kernel_spmd(nc, [arrays], core_ids=[0])
    return r.results[0]["out_h"]
```

```python
import concourse.bass as bass
from concourse import mybir
from contextlib import ExitStack

F32 = mybir.dt.float32
BF16 = mybir.dt.bfloat16
I32 = mybir.dt.int32
U32 = mybir.dt.uint32
ALU = mybir.AluOpType
ACT = mybir.ActivationFunctionType
AX = mybir.AxisListType

P = 128
S = 512
D = 1024
NT = S // P
KD = D // P
DA = 512
GA = 4
H, DH = 8, 64
E, FF = 32, 256
NG, EPG = 4, 8
BLK = 64
RING = 6
NPAIR = E // 2
PAIRS = 2 * S
NR = NPAIR + (PAIRS - 1) // BLK + 2
N_SMALL = 13
EPS = 1e-6
NEG = -1e30
BIG = 3e38
MAGIC = float(0x5F3759DF)


def hybrid_layer(nc, x, p, g_mix, w_in, g_v_a, w_s, b_s, g_q, g_k, g_out_a, g_out_b, w_out, g_ffn,
                 w_group, w_expert, w_gate_e, w_up_e, w_down_e, g_ple, w_ple, w_ple_gate, out):
    x_v = x[0].rearrange("(t p) d -> t p d", p=P)
    out_v = out[0].rearrange("(t p) d -> t p d", p=P)
    p_v = p[0, 0].rearrange("(t p) d -> p t d", p=P)
    win_v = w_in[0].rearrange("(p k) n -> p k n", k=KD)
    wout_v = w_out[0].rearrange("(k p) n -> p k n", p=P)
    wple_v = w_ple[0].rearrange("(k p) n -> p k n", p=P)
    wpg_v = w_ple_gate[0].rearrange("(p k) n -> p (k n)", k=KD)
    gate_v = w_gate_e[0].rearrange("e (p k) f -> e p (k f)", k=KD)
    up_v = w_up_e[0].rearrange("e (p k) f -> e p (k f)", k=KD)
    down_v = w_down_e[0].rearrange("e (c p) d -> e p c d", p=P)

    hn_dram = nc.dram_tensor("hn_rows", [S, D], F32, kind="Internal").ap()
    y_dram = nc.dram_tensor("y_rows", [PAIRS, D], F32, kind="Internal").ap()
    y_v = y_dram.rearrange("(k t p) d -> t p k d", k=2, p=P)

    ctx = ExitStack()
    with ctx:
        def sb(name, shape, dt=F32):
            return ctx.enter_context(nc.sbuf_tensor(name, shape, dt))

        def sem(name):
            return ctx.enter_context(nc.semaphore(name))

        h = sb("h", [P, NT, D])
        mem = sb("mem", [P, 3 * 12288 + 8960])
        slots = [mem[:, n * 6144:(n + 1) * 6144].rearrange("p (a b) -> p a b", a=3) for n in range(RING)]
        a1 = mem[:, 12288:24576]
        a2 = mem[:, 24576:36864]
        work = mem[:, 36864:]
        xnT = a1[:, 0:4096].rearrange("p (k t) -> p k t", k=KD)
        qTz = a1[:, 0:4096].rearrange("p (h t) -> p h t", h=H)
        u_a, v_a, q_b, k_b = (a1[:, 4096 + 2048 * c:6144 + 2048 * c].rearrange("p (t n) -> p t n", t=NT)
                              for c in range(4))
        ysq = a1[:, 8192:10240].rearrange("p (j t) -> p j t", j=4)
        hnT = a1[:, 8192:12288].rearrange("p (k t) -> p k t", k=KD)
        win = a2[:, 0:8192].rearrange("p (b k n) -> p b k n", b=2, k=KD)
        wout = a2[:, 0:8192].rearrange("p (k n) -> p k n", k=KD)
        kT = a2[:, 8192:10240].rearrange("p (j t) -> p j t", j=4)
        v_b = a2[:, 10240:12288].rearrange("p (t n) -> p t n", t=NT)
        wple = a2[:, 8192:10240].rearrange("p (k n) -> p k n", k=2)
        p_sb = a2[:, 10240:11264].rearrange("p (t n) -> p t n", t=NT)
        pT = a2[:, 11264:12288].rearrange("p (k t) -> p k t", k=2)
        chunks = (u_a, v_a, q_b, k_b, v_b)
        yT = work[:, 0:4096].rearrange("p (k t) -> p k t", k=8)
        pW = work[:, 0:4096].rearrange("p (t n) -> p t n", t=NT)
        probs = work[:, 4096:6144].rearrange("p (i k) -> p i k", i=NT)
        PT = work[:, 6144:8704].rearrange("p (b c q) -> p b c q", b=2, c=10)
        xs = work[:, 6144:8192].rearrange("p (b d) -> p b d", b=2)
        junk = work[:, 5120:6144]
        sqs = work[:, 4096:4608]
        wsT = work[:, 4608:5120].rearrange("p (g t) -> p g t", g=GA)
        wsb = work[:, 8192:8704].rearrange("p (g s) -> p g s", g=GA)
        xg = work[:, 4096:5120]
        xgT = work[:, 5120:6144].rearrange("p (k s) -> p k s", k=KD)
        ysb = work[:, 6144:7168]
        sil = work[:, 8192:8448].rearrange("p (b f) -> p b f", b=2)
        act = work[:, 8448:8704].rearrange("p (b f) -> p b f", b=2)
        aT = work[:, 8704:8960].rearrange("p (b f) -> p b f", b=2)
        wpg = a1[:, 0:8192].rearrange("p (k n) -> p k n", k=KD)
        yg = [a2[:, b * 2048:(b + 1) * 2048].rearrange("p (k d) -> p k d", k=2) for b in range(2)]
        hpT = a2[:, 4096:6144].rearrange("p (b k t) -> p b k t", b=2, k=KD)
        sg = a2[:, 6144:7168].rearrange("p (b n) -> p b n", b=2)
        gva = sb("gva", [P, DA])

        ident = sb("ident", [P, P])
        causal = sb("causal", [P, P])
        earlier = sb("earlier", [P, P], BF16)
        ones_b = sb("ones_b", [P, P], BF16)
        ones1 = sb("ones1", [P, 1])
        g3 = sb("g3", [P, 3, KD])
        gqk = sb("gqk", [P, 2])
        goab = sb("goab", [P, 8])
        bs = sb("bs", [P, GA])
        wr = sb("wr", [P, KD, NG + E])
        ss3 = sb("ss3", [P, 3, NT])
        rs = sb("rs", [P, 3, NT])
        ssn = sb("ssn", [P, 3, 32])
        rsn = sb("rsn", [P, 3, 32])
        ssab = sb("ssab", [P, 2, NT])
        rsab = sb("rsab", [P, 2, NT])
        rt = sb("rt", [P, 32])
        mx = sb("mx", [P, H * NT])
        nmx = sb("nmx", [P, H * NT])
        rsum = sb("rsum", [P, H * NT])
        rrec = sb("rrec", [P, H * NT])
        scratch = a2[:, 0:4096]
        used = [0]

        def tmp(*shape, rows=P, dt=F32):
            n, at = 1, used[0]
            for d in shape:
                n *= d
            used[0] += n
            assert used[0] <= 4096
            v = scratch[0:rows, at:at + n]
            if dt is not F32:
                v = v.bitcast(dt)
            names = "abc"[:len(shape)]
            return v.rearrange(f"p ({' '.join(names)}) -> p {' '.join(names)}", **dict(zip(names, shape)))

        lgT = tmp(S, rows=NG + E)
        lg = tmp(NT, NG + E)
        r4 = tmp(NT, 4)
        oh_g = tmp(NT, NG)
        r32 = tmp(NT, E)
        s32 = tmp(NT, E)
        r8 = tmp(NT, EPG)
        t8 = tmp(NT, EPG)
        oh1 = tmp(NT, EPG)
        oh2 = tmp(NT, EPG)
        m12 = tmp(4, NT)
        M1 = tmp(NT, E)
        M2 = tmp(NT, E)
        cnt = tmp(E)
        cmp8 = tmp(E, EPG)
        chunks_of = tmp(E)
        nr = tmp(NPAIR)
        incl = tmp(NPAIR)
        base = tmp(NPAIR)
        z0 = tmp(E)
        Ri = tmp(NT, E, dt=I32)
        Fi = tmp(NT, E, dt=I32)
        posf = tmp(2, NT)
        posi = tmp(2, NT, dt=I32)
        rndi = tmp(2, NT, dt=I32)
        rowf = tmp(2 * NT)
        rndf = tmp(2 * NT)
        ohs = tmp(2 * NT, P)
        ohb = tmp(2 * NT, NR)
        tbl = tmp(NR)
        tb2 = tmp(NR)
        regf = tmp(49)
        Mb = sb("Mb", [P, NT, E], BF16)
        cw = sb("cw", [P, 2, NT])
        gidx = sb("gidx", [P, NR], U32)
        sidx = sb("sidx", [P, NR], U32)
        gcol = sb("gcol", [P, 1], U32)
        scol = sb("scol", [P, 1], U32)
        regs = sb("regs", [P, 49], I32)
        rowv = sb("rowv", [P, 2, NT])
        n64 = sb("n64", [P, EPG])
        odd64 = sb("odd64", [P, NPAIR, 2])
        first = sb("first", [P, EPG])
        slf = sb("slf", [P, P])

        ps = [ctx.enter_context(nc.psum_tensor(f"ps{i}", [P, 512], F32)) for i in range(8)]

        ld_x = [sem(f"ld_x{t}") for t in range(NT)]
        ld_gain = sem("ld_gain")
        ld_small = sem("ld_small")
        ld_win = [sem(f"ld_win{b}") for b in range(2)]
        ld_wout = [sem(f"ld_wout{b}") for b in range(2)]
        ld_ple = sem("ld_ple")
        ld_gu = [sem(f"ld_gu{b}") for b in range(RING)]
        ld_down = [sem(f"ld_down{b}") for b in range(RING)]
        ld_wpg = sem("ld_wpg")
        ld_xg = sem("ld_xg")
        ld_yg = [sem(f"ld_yg{b}") for b in range(2)]
        st_hn = [sem(f"st_hn{b}") for b in range(2)]
        st_y = sem("st_y")
        st_out = sem("st_out")
        consts = sem("consts")
        sq_done = [sem(f"sq_done{k}") for k in range(3)]
        xs_ready = [sem(f"xs_ready{k}") for k in range(3)]
        xt_done = [sem(f"xt_done{k}") for k in range(3)]
        nT_ready = [sem(f"nT_ready{k}") for k in range(3)]
        ws_done = sem("ws_done")
        ws_ready = sem("ws_ready")
        proj_done = sem("proj_done")
        proj_ev = sem("proj_ev")
        qk_ready = sem("qk_ready")
        v_ready = sem("v_ready")
        kt_done = sem("kt_done")
        kt_ready = sem("kt_ready")
        qt_done = sem("qt_done")
        qt_ready = [sem(f"qt_ready{b}") for b in range(2)]
        qz_zero = sem("qz_zero")
        mix_done = sem("mix_done")
        ya_ready = sem("ya_ready")
        sa_done = sem("sa_done")
        ya_scaled = sem("ya_scaled")
        yat_done = sem("yat_done")
        yat_ready = sem("yat_ready")
        s_done = sem("s_done")
        nmx_ready = sem("nmx_ready")
        exp_done = sem("exp_done")
        p_ready = sem("p_ready")
        pt_done = sem("pt_done")
        pt_ready = sem("pt_ready")
        pv_done = sem("pv_done")
        yb_ready = sem("yb_ready")
        ysq_ready = sem("ysq_ready")
        sb_done = sem("sb_done")
        sb_read = sem("sb_read")
        wo_done = sem("wo_done")
        h_ready = sem("h_ready")
        lgt_done = sem("lgt_done")
        lgt_ready = sem("lgt_ready")
        lg_done = sem("lg_done")
        ex_in = sem("ex_in")
        ex_out = sem("ex_out")
        mb_ready = sem("mb_ready")
        rank_done = sem("rank_done")
        oh_ready = sem("oh_ready")
        idx_done = sem("idx_done")
        idx_ready = sem("idx_ready")
        pp_done = sem("pp_done")
        pp_ready = sem("pp_ready")
        pw_done = sem("pw_done")
        pw_ready = sem("pw_ready")
        xgt_done = sem("xgt_done")
        xgt_ready = sem("xgt_ready")
        gu_done = sem("gu_done")
        sil_ready = sem("sil_ready")
        act_ready = sem("act_ready")
        at_done = sem("at_done")
        at_ready = sem("at_ready")
        block_done = sem("block_done")
        ysb_ready = sem("ysb_ready")
        h2_ready = sem("h2_ready")
        pg_done = sem("pg_done")
        sg_ready = sem("sg_ready")
        sg_used = sem("sg_used")
        out_ready = sem("out_ready")
        dve_step = sem("dve_step")
        pool_step = sem("pool_step")
        column_ready = sem("column_ready")

        ORDER = [2, 3, 1, 4, 0]
        block = ctx.enter_context(nc.Block())

        @block.sync
        def _(sp):
            def load_expert(slot, gate, up, down):
                sp.dma_start(slots[slot][:, 0], gate).then_inc(ld_gu[slot], 16)
                sp.dma_start(slots[slot][:, 1], up).then_inc(ld_gu[slot], 16)
                sp.dma_start(slots[slot][:, 2].rearrange("p (c d) -> p c d", c=2), down).then_inc(ld_down[slot], 16)

            def load_static(e):
                load_expert(e % RING, gate_v[e], up_v[e], down_v[e])

            def load_at(slot, e):
                load_expert(slot, gate_v[bass.ds(e, 1)].rearrange("a p n -> p (a n)"),
                            up_v[bass.ds(e, 1)].rearrange("a p n -> p (a n)"),
                            down_v[bass.ds(e, 1)].rearrange("a p c d -> p (a c) d"))

            for t in range(NT):
                sp.dma_start(h[:, t], x_v[t]).then_inc(ld_x[t], 16)
            for n in range(2):
                sp.dma_start(win[:, n], win_v[:, :, ORDER[n] * 512:ORDER[n] * 512 + 512]).then_inc(ld_win[n], 16)
            load_static(0)
            load_static(1)
            for n in range(2, 5):
                sp.wait_ge(proj_done, NT * (n - 1))
                sp.dma_start(win[:, n % 2], win_v[:, :, ORDER[n] * 512:ORDER[n] * 512 + 512])\
                    .then_inc(ld_win[n % 2], 16)
            for b, n in ((1, 3), (0, 4)):
                sp.wait_ge(proj_done, NT * (n + 1))
                sp.dma_start(wout[:, 4 * b:4 * b + 4], wout_v[:, 4 * b:4 * b + 4]).then_inc(ld_wout[b], 16)
            sp.wait_ge(pv_done, H)
            sp.dma_start(wple, wple_v).then_inc(ld_ple, 16)
            sp.dma_start(p_sb, p_v).then_inc(ld_ple, 16)
            sp.wait_ge(yat_done, NT)
            load_static(2)
            for t in range(NT):
                sp.wait_ge(xs_ready[1], t + 1)
                sp.dma_start(hn_dram[t * P:t * P + P], xs[:, t % 2]).then_inc(st_hn[t % 2], 16)
            sp.wait_ge(lgt_done, 1)
            load_static(3)
            sp.wait_ge(idx_ready, 1)
            load_static(4)
            sp.wait_ge(pw_done, 2 * NT)
            load_static(5)
            with sp.Fori(0, 4) as i:
                for s in range(3):
                    used_at = sp.value_load(regs[0:1, bass.ds(3 * i + (NPAIR + s), 1)], min_val=2, max_val=2 * NR)
                    sp.wait_ge(block_done, used_at + 2)
                    for w in range(2):
                        sp.wait_ge(ld_gu[(2 * s + w - 1) % RING], 32 * i + (64 if s + w else 32))
                        load_at(2 * s + w, 6 * i + (6 + 2 * s + w))
            for q in (NPAIR - 4, NPAIR - 3):
                used_at = sp.value_load(regs[0:1, NPAIR + q:NPAIR + q + 1], min_val=2, max_val=2 * NR)
                sp.wait_ge(block_done, used_at + 2)
                if q == NPAIR - 4:
                    for w in range(2):
                        sp.wait_ge(ld_gu[(E - 3 + w) % RING], 32 * ((E - 3 + w) // RING + 1))
                        load_static(E - 2 + w)
                else:
                    sp.dma_start(wpg, wpg_v.rearrange("p (k n) -> p k n", k=KD)).then_inc(ld_wpg, 16)
            rounds = sp.value_load(regs[0:1, 48:49], min_val=NPAIR, max_val=NR - 2)
            sp.wait_ge(st_y, 16 * rounds)
            for t in range(NT):
                if t >= 2:
                    sp.wait_ge(h2_ready, 2 * (t - 1))
                sp.dma_start(yg[t % 2], y_v[t]).then_inc(ld_yg[t % 2], 16)
            for t in range(NT):
                sp.wait_ge(out_ready, t + 1)
                sp.dma_start(out_v[t], h[:, t]).then_inc(st_out, 16)
            sp.wait_ge(st_out, 16 * NT)

        @block.gpsimd
        def _(pool):
            steps = [0]

            def link(ins):
                steps[0] += 1
                ins.then_inc(pool_step, 1)
                pool.wait_ge(pool_step, steps[0])

            link(pool.memset(ident[:, :], 0.0))
            link(pool.affine_select(out=ident[:, :], in_=ident[:, :], compare_op=ALU.not_equal, fill=1.0, base=0,
                                    pattern=[[-1, P]], channel_multiplier=1))
            link(pool.memset(causal[:, :], 0.0))
            link(pool.affine_select(out=causal[:, :], in_=causal[:, :], compare_op=ALU.is_ge, fill=NEG, base=0,
                                    pattern=[[-1, P]], channel_multiplier=1))
            link(pool.memset(ones_b[:, :], 1.0))
            link(pool.affine_select(out=earlier[:, :], in_=ones_b[:, :], compare_op=ALU.is_gt, fill=0.0, base=0,
                                    pattern=[[1, P]], channel_multiplier=-1))
            for dst, pattern, first_value, mult in ((rowv, [[S, 2], [P, NT]], 1, 1), (n64, [[BLK, EPG]], 0, 0),
                                                    (odd64, [[0, NPAIR], [BLK, 2]], 0, 0),
                                                    (first, [[-1, EPG]], EPG, 0), (slf, [[1, P]], 0, 0)):
                link(pool.iota(dst[:], pattern=pattern, base=first_value, channel_multiplier=mult,
                               allow_small_or_imprecise_dtypes=True))
            pool.memset(ones1[:, :], 1.0).then_inc(consts, 1)
            pool.wait_ge(ws_ready, 1)
            pool.affine_select(out=wsT, in_=wsT, compare_op=ALU.is_ge, fill=0.0, base=0,
                               pattern=[[0, GA], [1, P]], channel_multiplier=-1).then_inc(ws_ready, 1)
            pool.wait_ge(ws_ready, 2)
            pool.wait_ge(proj_done, 5 * NT)
            pool.memset(qTz[64:128].rearrange("p (j b) t -> p j b t", b=2)[:, :, 0], 0.0).then_inc(qz_zero, 1)
            pool.wait_ge(qz_zero, 1)
            pool.memset(qTz[0:64].rearrange("p (j b) t -> p j b t", b=2)[:, :, 1], 0.0).then_inc(qz_zero, 1)
            pool.wait_ge(idx_ready, 1)
            for b in range(2):
                pool.wait_ge(st_hn[b], 32)
            rounds = pool.value_load(regs[0:1, 48:49], min_val=NPAIR, max_val=NR - 2)
            pool.indirect_dma_start(out=xg, out_offset=None, in_=hn_dram,
                                    in_offset=bass.IndirectOffsetOnAxis(ap=gidx[:, 0:1], axis=0)).then_inc(ld_xg, 16)
            pool.wait_ge(xgt_done, 2)
            pool.indirect_dma_start(out=xg, out_offset=None, in_=hn_dram,
                                    in_offset=bass.IndirectOffsetOnAxis(ap=gidx[:, 1:2], axis=0)).then_inc(ld_xg, 16)
            with pool.Fori(0, rounds) as r:
                pool.wait_ge(xgt_done, 2 * r + 4)
                pool.tensor_copy(gcol[:, :], gidx[:, bass.ds(r + 2, 1)]).then_inc(column_ready, 1)
                pool.wait_ge(column_ready, 1)
                pool.sem_clear(column_ready)
                pool.indirect_dma_start(out=xg, out_offset=None, in_=hn_dram,
                                        in_offset=bass.IndirectOffsetOnAxis(ap=gcol[:, :], axis=0))\
                    .then_inc(ld_xg, 16)
                pool.wait_ge(ysb_ready, 2 * r + 4)
                pool.tensor_copy(scol[:, :], sidx[:, bass.ds(r, 1)]).then_inc(column_ready, 1)
                pool.wait_ge(column_ready, 1)
                pool.sem_clear(column_ready)
                pool.indirect_dma_start(out=y_dram, out_offset=bass.IndirectOffsetOnAxis(ap=scol[:, :], axis=0),
                                        in_=ysb, in_offset=None, bounds_check=PAIRS - 1, oob_is_err=False)\
                    .then_inc(st_y, 16)

        @block.tensor
        def _(pe):
            mm = nc.tensor.matmul

            def transposes_of_tile(k, t, bank=None):
                pe.wait_ge(xs_ready[k], t + 1)
                back = 2 if k == 0 else 1
                if t >= back:
                    pe.wait_ge(nT_ready[k], t - back + 1)
                rows = xs[:, t % 2].rearrange("p (a k) -> p k a", k=KD)
                bank = 2 * (t % 2) if k == 0 else 4
                for j in range(KD):
                    last = nc.tensor.transpose(ps[bank + j // 4][:, j % 4 * P:j % 4 * P + P], rows[:, j], ident[:, :])
                last.then_inc(xt_done[k], 1)

            pe.wait_ge(consts, 1)

            def project(n, t):
                m = n * NT + t
                if n == 0:
                    pe.wait_ge(nT_ready[0], t + 1)
                if t == 0 or n == 0:
                    pe.wait_ge(ld_win[n % 2], 16 * (n // 2 + 1))
                if m >= 2:
                    pe.wait_ge(proj_ev, m - 1)
                for k in range(KD):
                    last = mm(ps[4 + m % 2][:, :], xnT[:, k, t * P:t * P + P], win[:, n % 2, k],
                              start=(k == 0), stop=(k == KD - 1))
                last.then_inc(proj_done, 1)

            transposes_of_tile(0, 0)
            for t in range(NT):
                if t + 1 < NT:
                    transposes_of_tile(0, t + 1)
                project(0, t)
            pe.wait_ge(ld_small, 16 * N_SMALL)
            for g in range(GA):
                last = nc.tensor.transpose(ps[6][:, g * P:g * P + P], wsb[:, g], ident[:, :])
            last.then_inc(ws_done, 1)
            for n in range(1, 5):
                for t in range(NT):
                    project(n, t)
                    if n == 3:
                        pe.wait_ge(qk_ready, NT + t + 1)
                        if t >= 2:
                            pe.wait_ge(kt_ready, t - 1)
                        for j in range(4):
                            last = nc.tensor.transpose(ps[t % 2][:, j * P:j * P + P], k_b[:, t, j * P:j * P + P],
                                                       ident[:, :])
                        last.then_inc(kt_done, 1)
            pe.wait_ge(kt_ready, NT)
            pe.wait_ge(qz_zero, 2)
            for t in range(NT):
                for j in range(4):
                    last = nc.tensor.transpose(ps[t][:, j * P:j * P + P], q_b[:, t, j * P:j * P + P], ident[:, :])
                last.then_inc(qt_done, 1)
            pe.wait_ge(ws_ready, 2)
            pe.wait_ge(v_ready, NT)
            for g in range(GA):
                if g >= 2:
                    pe.wait_ge(ya_ready, g - 1)
                mm(ps[6 + g % 2][:, :], wsT[:, g], v_a[:, :, g * P:g * P + P], start=True, stop=True)\
                    .then_inc(mix_done, 1)

            def scores(hh, i):
                n = hh * NT + i
                if hh:
                    pe.wait_ge(exp_done, n - NT + 1)
                mm(ps[i][:, 0:(i + 1) * P], qTz[:, hh, i * P:i * P + P], kT[:, hh // 2, 0:(i + 1) * P],
                   start=True, stop=True).then_inc(s_done, 1)

            for b in range(2):
                pe.wait_ge(qt_ready[b], NT)
            pe.wait_ge(proj_ev, 5 * NT)
            for i in range(NT):
                scores(0, i)
            for hh in range(H):
                for i in range(NT):
                    n = hh * NT + i
                    if hh + 1 < H:
                        scores(hh + 1, i)
                    pe.wait_ge(p_ready, n + 1)
                    if n >= 2:
                        pe.wait_ge(pt_ready, n - 1)
                    for kt in range(i + 1):
                        last = nc.tensor.transpose(ps[4 + n % 2][:, kt * P:kt * P + P], probs[:, i, kt * P:kt * P + P],
                                                   ident[:, :])
                    last.then_inc(pt_done, 1)
                pe.wait_ge(pt_ready, NT * (hh + 1))
                if hh % 2 == 0:
                    if hh >= 4:
                        pe.wait_ge(yb_ready, hh // 2 - 1)
                        pe.wait_ge(ysq_ready, hh // 2 - 1)
                    else:
                        pe.wait_ge(ya_ready, GA)
                rows = slice(64 * (hh % 2), 64 * (hh % 2) + 64)
                for i in range(NT):
                    for kt in range(i + 1):
                        last = mm(ps[6 + hh // 2 % 2][rows, i * P:i * P + P], v_b[:, kt, hh * DH:hh * DH + DH],
                                  PT[:, hh % 2, i * (i + 1) // 2 + kt], start=(kt == 0), stop=(kt == i))
                last.then_inc(pv_done, 1)
            for t in range(NT):
                pe.wait_ge(ya_scaled, t + 1)
                if t >= 2:
                    pe.wait_ge(yat_ready, t - 1)
                elif t == 0:
                    pe.wait_ge(pt_ready, H * NT)
                for j in range(4):
                    last = nc.tensor.transpose(ps[4 + t % 2][:, j * P:j * P + P], u_a[:, t, j * P:j * P + P], ident[:, :])
                last.then_inc(yat_done, 1)
            def squares_of_y_b():
                pe.wait_ge(ysq_ready, 4)
                for t in range(NT):
                    for j in range(4):
                        last = mm(ps[6][:, t:t + 1], ysq[:, j, t * P:t * P + P], ones1[:, :],
                                  start=(j == 0), stop=(j == 3))
                last.then_inc(sb_done, 1)

            pe.wait_ge(ld_wout[0], 16)
            pe.wait_ge(ld_wout[1], 16)
            pe.wait_ge(yat_ready, NT)

            def output_rows(t):
                for half in range(2):
                    n = 2 * t + half
                    if n >= 2:
                        pe.wait_ge(h_ready, n - 1)
                    if n == 0:
                        pe.wait_ge(exp_done, H * NT)
                    for w in range(2):
                        for k in range(4):
                            last = mm(ps[2 * (n % 2) + w][:, :], yT[:, 4 * w + k, t * P:t * P + P],
                                      wout[:, 4 * w + k, half * 512:half * 512 + 512], start=(k == 0), stop=(k == 3))
                    last.then_inc(wo_done, 1)

            pe.wait_ge(yb_ready, 4)
            for t in range(NT):
                output_rows(t)
                if t == 0:
                    squares_of_y_b()
                else:
                    transposes_of_tile(1, t - 1)
            pe.wait_ge(ld_ple, 32)

            def embedding(t):
                pe.wait_ge(pp_ready, t + 1)
                for half in range(2):
                    n = 2 * t + half
                    if n >= 2:
                        pe.wait_ge(pw_ready, n - 1)
                    for k in range(2):
                        last = mm(ps[n % 2][:, :], pT[:, k, t * P:t * P + P], wple[:, k, half * 512:half * 512 + 512],
                                  start=(k == 0), stop=(k == 1))
                    last.then_inc(pw_done, 1)

            for t in range(NT):
                if t:
                    pe.wait_ge(pp_ready, t)
                for k in range(2):
                    last = nc.tensor.transpose(ps[7][:, k * P:k * P + P], p_sb[:, t, k * P:k * P + P], ident[:, :])
                last.then_inc(pp_done, 1)
            transposes_of_tile(1, NT - 1)
            pe.wait_ge(nT_ready[1], NT)
            pe.wait_ge(sb_read, 1)
            for k in range(KD):
                last = mm(ps[6][0:NG + E, :], wr[:, k], hnT[:, k], start=(k == 0), stop=(k == KD - 1))
            last.then_inc(lgt_done, 1)
            pe.wait_ge(lgt_ready, 1)
            for t in range(NT):
                last = nc.tensor.transpose(ps[4][:, t * (NG + E):(t + 1) * (NG + E)], lgT[:, t * P:t * P + P],
                                           ident[0:NG + E, 0:NG + E])
            last.then_inc(lg_done, 1)
            pe.wait_ge(h_ready, 2 * NT)
            embedding(0)
            pe.wait_ge(mb_ready, 1)
            for t in range(NT):
                for t2 in range(t + 1):
                    mm(ps[5][:, t * E:t * E + E], (earlier if t2 == t else ones_b)[:, :], Mb[:, t2],
                       start=(t2 == 0), stop=(t2 == t))
            for t2 in range(NT):
                last = mm(ps[5][:, NT * E:NT * E + E], ones_b[:, :], Mb[:, t2], start=(t2 == 0), stop=(t2 == NT - 1))
            last.then_inc(rank_done, 1)
            embedding(1)
            pe.wait_ge(oh_ready, 1)
            for n in range(2 * NT):
                last = mm(ps[6][:, 0:NR], ohs[:, n], ohb[:, n],
                          start=(n == 0), stop=(n == 2 * NT - 1))
            last.then_inc(idx_done, 1)
            embedding(2)
            embedding(3)
            pe.wait_ge(idx_ready, 1)

            def transpose_half(half, n):
                rows = xg.rearrange("p (a k) -> p k a", k=KD)
                pe.wait_ge(ld_xg, n)
                for k in range(4):
                    last = nc.tensor.transpose(ps[6 + half][:, k * P:k * P + P], rows[:, 4 * half + k], ident[:, :])
                last.then_inc(xgt_done, 1)

            def expert_round(n, pair, loaded):
                pe.wait_ge(xgt_ready, n + 2)
                for s in range(2):
                    w = slots[2 * pair + s]
                    pe.wait_ge(ld_gu[2 * pair + s], 32 * loaded)
                    pe.wait_ge(act_ready, n + (s + 1))
                    for k in range(KD):
                        for c in range(2):
                            last = mm(ps[s][64 * c:64 * c + 64, 0:256], xgT[:, k, s * BLK:s * BLK + BLK],
                                      w[:, 0:2, k * FF + c * P:k * FF + c * P + P], start=(k == 0), stop=(k == KD - 1))
                    last.then_inc(gu_done, 1)
                for s in range(2):
                    w = slots[2 * pair + s]
                    pe.wait_ge(act_ready, n + (s + 3))
                    nc.tensor.transpose(ps[4][:, s * P:s * P + P], act[:, s], ident[:, :]).then_inc(at_done, 1)
                    transpose_half(s, 8 * n + 32)
                    pe.wait_ge(ld_down[2 * pair + s], 16 * loaded)
                    pe.wait_ge(at_ready, n + (s + 1))
                    pe.wait_ge(ysb_ready, n + (s + 1))
                    for c in range(2):
                        for half in range(2):
                            last = mm(ps[2 + s][64 * half:64 * half + 64, :], aT[:, s, c * 64:c * 64 + 64],
                                      w[:, 2, c * D + half * 512:c * D + half * 512 + 512],
                                      start=(c == 0), stop=(c == 1))
                    last.then_inc(block_done, 1)

            def pair_rounds(q, pair, loaded):
                rounds = pe.value_load(regs[0:1, bass.ds(q, 1)], min_val=1, max_val=S // BLK)
                before = pe.value_load(regs[0:1, bass.ds(q + 2 * NPAIR, 1)], min_val=0, max_val=2 * NR)
                with pe.Fori(0, rounds) as k:
                    expert_round(before + 2 * k, pair, loaded)

            pe.sem_inc(at_done, 2)
            pe.sem_inc(block_done, 2)
            pe.wait_ge(pw_ready, 2 * NT)
            for half in range(2):
                transpose_half(half, 16)
            with pe.Fori(0, NPAIR // 3) as i:
                for s in range(3):
                    pair_rounds(3 * i + s, s, i + 1)
            pair_rounds(NPAIR - 1, 0, NPAIR // 3 + 1)
            pe.wait_ge(ld_wpg, 16)
            for t in range(NT):
                transposes_of_tile(2, t)
                for half in range(2):
                    n = 2 * t + half
                    if half == 0:
                        pe.wait_ge(nT_ready[2], t + 1)
                    if n >= 2:
                        pe.wait_ge(sg_ready, n - 1)
                    for k in range(KD):
                        last = mm(ps[n % 2][:, :], hpT[:, t % 2, k], wpg[:, k, half * 512:half * 512 + 512],
                                  start=(k == 0), stop=(k == KD - 1))
                    last.then_inc(pg_done, 1)

        @block.scalar
        def _(act_e):
            e_ = nc.scalar

            def squares(k, t):
                e_.activation(junk, h[:, t], ACT.Square, accum_out=ss3[:, k, t:t + 1]).then_inc(sq_done[k], 1)
                act_e.wait_ge(sq_done[k], t + 1)

            small = [(wsb, w_s[0].rearrange("g t s -> t g s")),
                     (gva[:, :], g_v_a[0:1, :].broadcast_to([P, DA])),
                     (bs[:, :], b_s[0].rearrange("g t -> t g")),
                     (gqk[0:64, 0:1], g_q[0:1].rearrange("a d -> d a")),
                     (gqk[64:128, 0:1], g_q[0:1].rearrange("a d -> d a")),
                     (gqk[0:64, 1:2], g_k[0:1].rearrange("a d -> d a")),
                     (gqk[64:128, 1:2], g_k[0:1].rearrange("a d -> d a")),
                     (goab[:, 0:4], g_out_a[0].rearrange("(k p) -> p k", p=P)),
                     (goab[:, 4:8], g_out_b[0].rearrange("(k p) -> p k", p=P)),
                     (g3[:, 1], g_ffn[0].rearrange("(p k) -> p k", k=KD)),
                     (g3[:, 2], g_ple[0].rearrange("(p k) -> p k", k=KD)),
                     (wr[:, :, 0:NG], w_group[0].rearrange("(p k) n -> p k n", k=KD)),
                     (wr[:, :, NG:], w_expert[0].rearrange("(p k) n -> p k n", k=KD))]
            assert len(small) == N_SMALL
            act_e.dma_start(g3[:, 0], g_mix[0].rearrange("(p k) -> p k", k=KD)).then_inc(ld_gain, 16)
            for t in range(NT):
                act_e.wait_ge(ld_x[t], 16)
                squares(0, t)
            for dst, src in small:
                act_e.dma_start(dst, src, allow_slow_non_contiguous=True).then_inc(ld_small, 16)
            for n, c in enumerate(ORDER):
                for t in range(NT):
                    m = n * NT + t
                    act_e.wait_ge(proj_done, m + 1)
                    e_.activation(chunks[c][:, t], ps[4 + m % 2][:, :], ACT.Gelu_apprx_tanh if c < 2 else ACT.Copy)\
                        .then_inc(proj_ev, 1)
            for t in range(NT):
                act_e.wait_ge(qt_done, t + 1)
                e_.activation(qTz[64:128].rearrange("p (j b) t -> p j b t", b=2)[:, :, 1, t * P:t * P + P],
                              ps[t][64:128, :].rearrange("p (j t) -> p j t", j=4), ACT.Copy, scale=gqk[64:128, 0:1])\
                    .then_inc(qt_ready[1], 1)
            act_e.wait_ge(ya_ready, GA)
            for t in range(NT):
                e_.activation(junk[:, 0:DA], u_a[:, t], ACT.Square, accum_out=ssab[:, 0, t:t + 1]).then_inc(sa_done, 1)
                act_e.wait_ge(sa_done, t + 1)

            def exps(hh, i):
                n = hh * NT + i
                act_e.wait_ge(nmx_ready, n + 1)
                e_.activation(probs[:, i, 0:(i + 1) * P], ps[i][:, 0:(i + 1) * P], ACT.Exp, bias=nmx[:, n:n + 1],
                              scale=DH ** -0.5, accum_out=rsum[:, n:n + 1]).then_inc(exp_done, 1)

            for i in range(NT):
                exps(0, i)
            for hh in range(H):
                for i in range(NT):
                    n = hh * NT + i
                    act_e.wait_ge(pt_done, n + 1)
                    if hh >= 2:
                        act_e.wait_ge(pv_done, hh - 1)
                    e_.activation(PT[:, hh % 2, i * (i + 1) // 2:(i + 1) * (i + 2) // 2].rearrange("p a b -> p (a b)"),
                                  ps[4 + n % 2][:, 0:(i + 1) * P], ACT.Copy).then_inc(pt_ready, 1)
                    if hh + 1 < H:
                        exps(hh + 1, i)
                if hh % 2:
                    j = hh // 2
                    act_e.wait_ge(yb_ready, j + 1)
                    e_.activation(ysq[:, j], ps[6 + j % 2][:, :], ACT.Square).then_inc(ysq_ready, 1)
            for t in range(NT):
                act_e.wait_ge(h_ready, 2 * (t + 1))
                if t == 0:
                    act_e.wait_ge(pv_done, H)
                squares(1, t)
            for t in range(NT):
                act_e.wait_ge(pp_done, t + 1)
                e_.activation(pT[:, :, t * P:t * P + P], ps[7][:, 0:2 * P].rearrange("p (k t) -> p k t", k=2), ACT.Copy)\
                    .then_inc(pp_ready, 1)
            act_e.wait_ge(lgt_done, 1)
            e_.activation(lgT[:, :], ps[6][0:NG + E, :], ACT.Copy).then_inc(lgt_ready, 1)
            act_e.wait_ge(ex_in, 1)
            e_.activation(lg[:, :, 0:NG], lg[:, :, 0:NG], ACT.Exp).then_inc(ex_out, 1)
            act_e.wait_ge(ex_in, 2)
            e_.activation(m12[:, 2], m12[:, 1], ACT.Exp).then_inc(ex_out, 1)
            for n in range(2 * NT):
                act_e.wait_ge(pw_done, n + 1)
                e_.activation(pW[:, n // 2, n % 2 * 512:n % 2 * 512 + 512], ps[n % 2][:, :], ACT.Copy)\
                    .then_inc(pw_ready, 1)
            act_e.wait_ge(idx_ready, 1)
            rounds = act_e.value_load(regs[0:1, 48:49], min_val=NPAIR, max_val=NR - 2)
            act_e.sem_inc(ysb_ready, 2)

            def round_of_blocks(r, first):
                for s in range(2):
                    act_e.wait_ge(gu_done, 2 * r + (s + 1))
                    act_e.wait_ge(act_ready, 2 * r + (s + 1))
                    e_.activation(sil[:, s], ps[s][:, 0:P], ACT.Silu).then_inc(sil_ready, 1)
                for s in range(2):
                    act_e.wait_ge(block_done, 2 * r + (s + 3))
                    if s == 0 and not first:
                        act_e.wait_ge(st_y, 16 * r)
                    for half in range(2):
                        ins = e_.activation(ysb[s * BLK:s * BLK + BLK, half * 512:half * 512 + 512],
                                            ps[2 + s][64 * half:64 * half + 64, :], ACT.Copy)
                    ins.then_inc(ysb_ready, 1)

            round_of_blocks(0, True)
            with act_e.Fori(1, rounds) as r:
                round_of_blocks(r, False)

            def sigmoids(t):
                for half in range(2):
                    n = 2 * t + half
                    act_e.wait_ge(pg_done, n + 1)
                    if n >= 2:
                        act_e.wait_ge(sg_used, n - 1)
                    e_.activation(sg[:, n % 2], ps[n % 2][:, :], ACT.Sigmoid).then_inc(sg_ready, 1)

            for t in range(NT):
                act_e.wait_ge(h2_ready, 2 * (t + 1))
                squares(2, t)
                if t:
                    sigmoids(t - 1)
            sigmoids(NT - 1)

        @block.vector
        def _(dve):
            v = nc.vector
            steps = [0]

            def link(ins):
                steps[0] += 1
                ins.then_inc(dve_step, 1)
                dve.wait_ge(dve_step, steps[0])

            def rsqrt(dst, m, n, width):
                t = rt[:, 0:width]
                link(v.tensor_scalar(m, m, 1.0 / n, EPS, ALU.mult, ALU.add))
                link(v.tensor_scalar(dst.bitcast(I32), m.bitcast(I32), 1, None, ALU.logical_shift_right))
                link(v.tensor_scalar(dst.bitcast(I32), dst.bitcast(I32), -1.0, MAGIC, ALU.mult, ALU.add))
                for _ in range(3):
                    link(v.tensor_tensor(t, dst, dst, ALU.mult))
                    link(v.scalar_tensor_tensor(out=t, in0=t, scalar=-0.5, in1=m, op0=ALU.mult, op1=ALU.mult))
                    link(v.scalar_tensor_tensor(out=dst, in0=t, scalar=1.5, in1=dst, op0=ALU.add, op1=ALU.mult))

            def scaled_rows(k, t):
                dve.wait_ge(sq_done[k], t + 1)
                rsqrt(rs[:, k, t:t + 1], ss3[:, k, t:t + 1], D, 1)
                if t >= 2:
                    dve.wait_ge(xt_done[k], t - 1)
                    if k == 1:
                        dve.wait_ge(st_hn[t % 2], 16)
                v.tensor_scalar(xs[:, t % 2], h[:, t], rs[:, k, t:t + 1], None, ALU.mult).then_inc(xs_ready[k], 1)

            def normed(k, t, dst):
                dve.wait_ge(xt_done[k], t + 1)
                bank = 2 * (t % 2) if k == 0 else 4
                for b in range(2):
                    ins = v.tensor_tensor(dst[:, 4 * b:4 * b + 4],
                                          ps[bank + b][:, :].rearrange("p (k t) -> p k t", k=4),
                                          g3[:, k, 4 * b:4 * b + 4].unsqueeze(2).broadcast_to([P, 4, P]), ALU.mult)
                ins.then_inc(nT_ready[k], 1)

            dve.sem_inc(act_ready, 2)
            dve.wait_ge(ld_gain, 16)
            scaled_rows(0, 0)
            for t in range(NT):
                if t + 1 < NT:
                    scaled_rows(0, t + 1)
                normed(0, t, xnT[:, :, t * P:t * P + P])
            dve.wait_ge(ws_done, 1)
            v.tensor_copy(wsT.rearrange("p g t -> p (g t)"), ps[6][:, :]).then_inc(ws_ready, 1)
            for n, c in enumerate(ORDER[0:3]):
                w = DH if n < 2 else P
                m = DA // w
                for t in range(NT):
                    dve.wait_ge(proj_ev, n * NT + t + 1)
                    link(v.tensor_tensor(sqs, chunks[c][:, t], chunks[c][:, t], ALU.mult))
                    link(v.tensor_reduce(ssn[:, n, t * m:t * m + m], sqs.rearrange("p (a b) -> p a b", b=w),
                                         axis=AX.X, op=ALU.add))
                rsqrt(rsn[:, n, 0:NT * m], ssn[:, n, 0:NT * m], w, NT * m)
                for t in range(NT):
                    a = chunks[c][:, t].rearrange("p (a b) -> p a b", b=w)
                    ins = v.tensor_tensor(a, a, rsn[:, n, t * m:t * m + m].unsqueeze(2).broadcast_to([P, m, w]), ALU.mult)
                    if n < 2:
                        ins.then_inc(qk_ready, 1)
                    else:
                        link(ins)
                        v.tensor_tensor(v_a[:, t], v_a[:, t], gva[:, :], ALU.mult).then_inc(v_ready, 1)
            for t in range(NT):
                dve.wait_ge(kt_done, t + 1)
                v.tensor_scalar(kT[:, :, t * P:t * P + P], ps[t % 2][:, :].rearrange("p (j t) -> p j t", j=4),
                                gqk[:, 1:2], None, ALU.mult).then_inc(kt_ready, 1)
            for t in range(NT):
                dve.wait_ge(qt_done, t + 1)
                v.tensor_scalar(qTz[0:64].rearrange("p (j b) t -> p j b t", b=2)[:, :, 0, t * P:t * P + P],
                                ps[t][0:64, :].rearrange("p (j t) -> p j t", j=4), gqk[0:64, 0:1], None, ALU.mult)\
                    .then_inc(qt_ready[0], 1)
            dve.wait_ge(proj_ev, 5 * NT)
            for g in range(GA):
                dve.wait_ge(mix_done, g + 1)
                u = u_a[:, :, g * P:g * P + P]
                v.scalar_tensor_tensor(out=u, in0=ps[6 + g % 2][:, :].rearrange("p (n d) -> p n d", n=NT),
                                       scalar=bs[:, g:g + 1], in1=u, op0=ALU.add, op1=ALU.mult).then_inc(ya_ready, 1)

            def row_max(hh, i):
                n = hh * NT + i
                dve.wait_ge(s_done, n + 1)
                diag = ps[i][:, i * P:i * P + P]
                link(v.tensor_tensor(diag, diag, causal[:, :], ALU.add))
                link(v.tensor_reduce(mx[:, n:n + 1], ps[i][:, 0:(i + 1) * P], axis=AX.X, op=ALU.max))
                v.tensor_scalar(nmx[:, n:n + 1], mx[:, n:n + 1], -DH ** -0.5, None, ALU.mult).then_inc(nmx_ready, 1)

            for i in range(NT):
                row_max(0, i)
            dve.wait_ge(sa_done, NT)
            rsqrt(rsab[:, 0], ssab[:, 0], DA, NT)
            for t in range(NT):
                v.tensor_scalar(u_a[:, t], u_a[:, t], rsab[:, 0, t:t + 1], None, ALU.mult).then_inc(ya_scaled, 1)
            for hh in range(H):
                for i in range(NT):
                    n = hh * NT + i
                    dve.wait_ge(exp_done, n + 1)
                    link(v.reciprocal(rrec[:, n:n + 1], rsum[:, n:n + 1]))
                    v.tensor_scalar(probs[:, i, 0:(i + 1) * P], probs[:, i, 0:(i + 1) * P], rrec[:, n:n + 1], None,
                                    ALU.mult).then_inc(p_ready, 1)
                    if hh + 1 < H:
                        row_max(hh + 1, i)
                if hh % 2:
                    j = hh // 2
                    dve.wait_ge(pv_done, hh + 1)
                    v.tensor_scalar(yT[:, 4 + j], ps[6 + j % 2][:, :], goab[:, 4 + j:5 + j], None, ALU.mult)\
                        .then_inc(yb_ready, 1)
            for t in range(NT):
                dve.wait_ge(yat_done, t + 1)
                v.tensor_tensor(yT[:, 0:4, t * P:t * P + P], ps[4 + t % 2][:, :].rearrange("p (k t) -> p k t", k=4),
                                goab[:, 0:4].unsqueeze(2).broadcast_to([P, 4, P]), ALU.mult).then_inc(yat_ready, 1)
            dve.wait_ge(sb_done, 1)
            v.tensor_copy(ssab[:, 1], ps[6][:, 0:NT]).then_inc(sb_read, 1)
            dve.wait_ge(sb_read, 1)
            rsqrt(rsab[:, 1], ssab[:, 1], DA, NT)
            for t in range(NT):
                for half in range(2):
                    n = 2 * t + half
                    dve.wait_ge(wo_done, n + 1)
                    cols = h[:, t, half * 512:half * 512 + 512]
                    link(v.tensor_tensor(cols, cols, ps[2 * (n % 2)][:, :], ALU.add))
                    v.scalar_tensor_tensor(out=cols, in0=ps[2 * (n % 2) + 1][:, :], scalar=rsab[:, 1, t:t + 1], in1=cols,
                                           op0=ALU.mult, op1=ALU.add).then_inc(h_ready, 1)
                scaled_rows(1, t)
                if t:
                    normed(1, t - 1, hnT[:, :, (t - 1) * P:t * P])
            normed(1, NT - 1, hnT[:, :, (NT - 1) * P:NT * P])
            dve.wait_ge(lg_done, 1)
            link(v.tensor_copy(lg[:, :, :], ps[4][:, 0:NT * (NG + E)].rearrange("p (t n) -> p t n", t=NT)))

            def col(a):
                return a.unsqueeze(2)

            def one_hot_of_max(dst, src, top, n):
                link(v.tensor_reduce(top, src, axis=AX.X, op=ALU.max))
                link(v.tensor_tensor(dst, src, col(top).broadcast_to([P, NT, n]), ALU.is_equal))
                link(v.tensor_tensor(dst, dst, first[:, 0:n].unsqueeze(1).broadcast_to([P, NT, n]), ALU.mult))
                link(v.tensor_reduce(r4[:, :, 3], dst, axis=AX.X, op=ALU.max))
                link(v.tensor_tensor(dst, dst, col(r4[:, :, 3]).broadcast_to([P, NT, n]), ALU.is_equal))

            one_hot_of_max(oh_g[:, :, :], lg[:, :, 0:NG], r4[:, :, 0], NG)
            v.tensor_tensor(lg[:, :, 0:NG], lg[:, :, 0:NG], col(r4[:, :, 0]).broadcast_to([P, NT, NG]), ALU.subtract)\
                .then_inc(ex_in, 1)
            oh_gb = oh_g[:, :, :].unsqueeze(3).broadcast_to([P, NT, NG, EPG])
            l4 = s32[:, :, :].rearrange("p t (g e) -> p t g e", g=NG)
            for t in range(NT):
                link(v.tensor_tensor(l4[:, t], lg[:, t, NG:].rearrange("p (g e) -> p g e", g=NG), oh_gb[:, t], ALU.mult))
            link(v.tensor_reduce(r8[:, :, :], s32[:, :, :].rearrange("p t (g e) -> p t e g", g=NG), axis=AX.X, op=ALU.add))
            one_hot_of_max(oh1[:, :, :], r8[:, :, :], m12[:, 0], EPG)
            link(v.scalar_tensor_tensor(out=t8[:, :, :], in0=oh1[:, :, :], scalar=-BIG, in1=r8[:, :, :],
                                        op0=ALU.mult, op1=ALU.add))
            one_hot_of_max(oh2[:, :, :], t8[:, :, :], m12[:, 1], EPG)
            v.tensor_tensor(m12[:, 1], m12[:, 1], m12[:, 0], ALU.subtract).then_inc(ex_in, 1)
            for t in range(NT):
                for M, oh in ((M1, oh1), (M2, oh2)):
                    link(v.tensor_tensor(M[:, t].rearrange("p (g e) -> p g e", g=NG), oh_gb[:, t],
                                         oh[:, t:t + 1].broadcast_to([P, NG, EPG]), ALU.mult))
            v.tensor_tensor(Mb[:, :, :], M1[:, :, :], M2[:, :, :], ALU.add).then_inc(mb_ready, 1)
            dve.wait_ge(ex_out, 2)
            link(v.tensor_reduce(r4[:, :, 1], lg[:, :, 0:NG], axis=AX.X, op=ALU.add))
            link(v.tensor_scalar(m12[:, 3], m12[:, 2], 1.0, None, ALU.add))
            link(v.tensor_tensor(r4[:, :, 1], r4[:, :, 1], m12[:, 3], ALU.mult))
            link(v.reciprocal(cw[:, 0], r4[:, :, 1]))
            link(v.tensor_tensor(cw[:, 1], cw[:, 0], m12[:, 2], ALU.mult))
            dve.wait_ge(rank_done, 1)
            link(v.tensor_copy(r32[:, :, :], ps[5][:, 0:NT * E].rearrange("p (t e) -> p t e", t=NT)))
            link(v.tensor_copy(Ri[:, :, :], r32[:, :, :]))
            link(v.tensor_copy(cnt[:, :], ps[5][:, NT * E:NT * E + E]))
            link(v.tensor_tensor(cmp8[:, :, :], cnt[:, :].unsqueeze(2).broadcast_to([P, E, EPG]),
                                 n64[:, :].unsqueeze(1).broadcast_to([P, E, EPG]), ALU.is_gt))
            link(v.tensor_reduce(chunks_of[:, :], cmp8[:, :, :], axis=AX.X, op=ALU.add))
            link(v.tensor_reduce(nr[:, :], chunks_of[:, :].rearrange("p (q b) -> p q b", b=2), axis=AX.X, op=ALU.max))
            link(v.tensor_scalar(nr[:, :], nr[:, :], 1.0, None, ALU.max))
            link(v.tensor_tensor_scan(out=incl[:, :], data0=nr[:, :], data1=nr[:, :], initial=0.0,
                                      op0=ALU.add, op1=ALU.max))
            link(v.tensor_tensor(base[:, :], incl[:, :], nr[:, :], ALU.subtract))
            link(v.scalar_tensor_tensor(out=z0[:, :].rearrange("p (q b) -> p q b", b=2),
                                        in0=base[:, :].unsqueeze(2).broadcast_to([P, NPAIR, 2]), scalar=float(P),
                                        in1=odd64[:, :, :], op0=ALU.mult, op1=ALU.add))
            link(v.tensor_scalar(Fi[:, :, :], Ri[:, :, :], 6, None, ALU.logical_shift_right))
            link(v.tensor_scalar(Ri[:, :, :], Ri[:, :, :], BLK - 1, None, ALU.bitwise_and))
            link(v.scalar_tensor_tensor(out=r32[:, :, :], in0=Fi[:, :, :], scalar=float(P), in1=Ri[:, :, :],
                                        op0=ALU.mult, op1=ALU.add))
            link(v.tensor_tensor(r32[:, :, :], r32[:, :, :], z0[:, :].unsqueeze(1).broadcast_to([P, NT, E]), ALU.add))
            for k, M in ((0, M1), (1, M2)):
                link(v.tensor_tensor(s32[:, :, :], M[:, :, :], r32[:, :, :], ALU.mult))
                link(v.tensor_reduce(posf[:, k], s32[:, :, :], axis=AX.X, op=ALU.add))
            link(v.tensor_copy(posi[:, :, :], posf[:, :, :]))
            link(v.tensor_scalar(rndi[:, :, :], posi[:, :, :], 7, None, ALU.logical_shift_right))
            link(v.tensor_scalar(posi[:, :, :], posi[:, :, :], P - 1, None, ALU.bitwise_and))
            link(v.tensor_copy(rndf[:, :], rndi[:, :, :].rearrange("p k t -> p (k t)")))
            link(v.tensor_copy(rowf[:, :], posi[:, :, :].rearrange("p k t -> p (k t)")))
            link(v.tensor_tensor(ohb[:, :, :], slf[:, 0:NR].unsqueeze(1).broadcast_to([P, 2 * NT, NR]),
                                 rndf[:, :].unsqueeze(2).broadcast_to([P, 2 * NT, NR]), ALU.is_equal))
            link(v.tensor_tensor(ohb[:, :, :], ohb[:, :, :], rowv[:, :, :].rearrange("p k t -> p (k t)").unsqueeze(2)
                                 .broadcast_to([P, 2 * NT, NR]), ALU.mult))
            v.tensor_tensor(ohs[:, :, :], slf[:, :].unsqueeze(1).broadcast_to([P, 2 * NT, P]),
                            rowf[:, :].unsqueeze(2).broadcast_to([P, 2 * NT, P]), ALU.is_equal).then_inc(oh_ready, 1)
            link(v.tensor_copy(regf[:, 0:NPAIR], nr[:, :]))
            link(v.tensor_scalar(regf[:, NPAIR:2 * NPAIR], incl[:, :], 2.0, None, ALU.mult))
            link(v.tensor_scalar(regf[:, 2 * NPAIR:3 * NPAIR], base[:, :], 2.0, None, ALU.mult))
            link(v.tensor_copy(regf[:, 48:49], incl[:, NPAIR - 1:NPAIR]))
            link(v.tensor_copy(regs[:, :], regf[:, :]))
            dve.wait_ge(idx_done, 1)
            link(v.tensor_scalar(tbl[:, :], ps[6][:, 0:NR], -1.0, 0.0, ALU.add, ALU.max))
            link(v.tensor_scalar(tb2[:, :], ps[6][:, 0:NR], float(S), float(-S), ALU.is_gt, ALU.mult))
            link(v.tensor_tensor(gidx[:, :], tbl[:, :], tb2[:, :], ALU.add))
            link(v.tensor_scalar(tb2[:, :], ps[6][:, 0:NR], 0.0, float(4 * PAIRS), ALU.is_equal, ALU.mult))
            v.tensor_tensor(sidx[:, :], tbl[:, :], tb2[:, :], ALU.add).then_inc(idx_ready, 1)
            dve.wait_ge(idx_ready, 1)
            rounds = dve.value_load(regs[0:1, 48:49], min_val=NPAIR, max_val=NR - 2)

            def xgt_copy(m, half):
                dve.wait_ge(xgt_done, m)
                v.tensor_tensor(xgT[:, 4 * half:4 * half + 4], ps[6 + half][:, :].rearrange("p (k s) -> p k s", k=4),
                                g3[:, 1, 4 * half:4 * half + 4].unsqueeze(2).broadcast_to([P, 4, P]), ALU.mult)\
                    .then_inc(xgt_ready, 1)

            for half in range(2):
                xgt_copy(half + 1, half)
            with dve.Fori(0, rounds) as r:
                for s in range(2):
                    dve.wait_ge(sil_ready, 2 * r + (s + 1))
                    dve.wait_ge(at_done, 2 * r + (s + 1))
                    v.tensor_tensor(act[:, s], sil[:, s], ps[s][:, P:2 * P], ALU.mult).then_inc(act_ready, 1)
                for s in range(2):
                    dve.wait_ge(at_done, 2 * r + (s + 3))
                    dve.wait_ge(block_done, 2 * r + (s + 1))
                    v.tensor_copy(aT[:, s], ps[4][:, s * P:s * P + P]).then_inc(at_ready, 1)
                    xgt_copy(2 * r + (s + 3), s)
            def combine(t):
                dve.wait_ge(ld_yg[t % 2], 16 * (t // 2 + 1))
                for k in range(2):
                    v.scalar_tensor_tensor(out=h[:, t], in0=yg[t % 2][:, k], scalar=cw[:, k, t:t + 1], in1=h[:, t],
                                           op0=ALU.mult, op1=ALU.add).then_inc(h2_ready, 1)
                    dve.wait_ge(h2_ready, 2 * t + k + 1)

            def finish(t):
                for half in range(2):
                    n = 2 * t + half
                    dve.wait_ge(sg_ready, n + 1)
                    c = slice(half * 512, half * 512 + 512)
                    v.tensor_tensor(pW[:, t, c], pW[:, t, c], sg[:, n % 2], ALU.mult).then_inc(sg_used, 1)
                    dve.wait_ge(sg_used, n + 1)
                    last = v.tensor_tensor(h[:, t, c], h[:, t, c], pW[:, t, c], ALU.add)
                    if half == 0:
                        link(last)
                last.then_inc(out_ready, 1)

            for t in range(NT):
                combine(t)
                scaled_rows(2, t)
                if t:
                    finish(t - 1)
                normed(2, t, hpT[:, t % 2])
            finish(NT - 1)


_INS = ["x", "p", "g_mix", "w_in", "g_v_a", "w_s", "b_s", "g_q", "g_k", "g_out_a", "g_out_b", "w_out", "g_ffn",
        "w_group", "w_expert", "w_gate_e", "w_up_e", "w_down_e", "g_ple", "w_ple", "w_ple_gate"]


def kernel(**inputs):
    import numpy as np
    import concourse.bacc as bacc
    from concourse.bass_utils import run_bass_kernel_spmd

    nc = bacc.Bacc("TRN2", target_bir_lowering=False, num_devices=1)
    arrays, args = {}, []
    for name in _INS:
        a = np.ascontiguousarray(inputs[name])
        arrays[f"in_{name}"] = a
        args.append(nc.dram_tensor(f"in_{name}", a.shape, mybir.dt.from_np(a.dtype), kind="ExternalInput").ap())
    out = nc.dram_tensor("out_h", (1, S, D), F32, kind="ExternalOutput").ap()
    hybrid_layer(nc, *args, out)
    r = run_bass_kernel_spmd(nc, [arrays], core_ids=[0])
    return r.results[0]["out_h"]
```

```python
import concourse.bass as bass
from concourse import mybir
from contextlib import ExitStack

F32 = mybir.dt.float32
BF16 = mybir.dt.bfloat16
F32R = mybir.dt.float32r
I32 = mybir.dt.int32
U32 = mybir.dt.uint32
ALU = mybir.AluOpType
ACT = mybir.ActivationFunctionType
AX = mybir.AxisListType

P = 128
S = 512
D = 1024
NT = S // P
KD = D // P
DA = 512
GA = 4
H, DH = 8, 64
E, FF = 32, 256
NG, EPG = 4, 8
BLK = 64
RING = 6
NPAIR = E // 2
PAIRS = 2 * S
NR = NPAIR + (PAIRS - 1) // BLK + 1
N_SMALL = 13
EPS = 1e-6
NEG = -1e30
BIG = 3e38
SBUF_AT = 16640
MAGIC = float(0x5F3759DF)


def hybrid_layer(nc, x, p, g_mix, w_in, g_v_a, w_s, b_s, g_q, g_k, g_out_a, g_out_b, w_out, g_ffn,
                 w_group, w_expert, w_gate_e, w_up_e, w_down_e, g_ple, w_ple, w_ple_gate, out):
    x_v = x[0].rearrange("(t p) d -> t p d", p=P)
    out_v = out[0].rearrange("(t p) d -> t p d", p=P)
    p_v = p[0, 0].rearrange("(t p) d -> p t d", p=P)
    win_v = w_in[0].rearrange("(p k) n -> p k n", k=KD)
    wout_v = w_out[0].rearrange("(k p) n -> p k n", p=P)
    wple_v = w_ple[0].rearrange("(k p) n -> p k n", p=P)
    wpg_v = w_ple_gate[0].rearrange("(p k) n -> p (k n)", k=KD)
    gate_v = w_gate_e[0].rearrange("e (p k) f -> e p (k f)", k=KD)
    up_v = w_up_e[0].rearrange("e (p k) f -> e p (k f)", k=KD)
    down_v = w_down_e[0].rearrange("e (c p) d -> e p c d", p=P)

    hn_dram = nc.dram_tensor("hn_rows", [S, D], F32, kind="Internal").ap()
    y_dram = nc.dram_tensor("y_rows", [PAIRS, D], F32, kind="Internal").ap()
    y_v = y_dram.rearrange("(k t p) d -> t p k d", k=2, p=P)

    ctx = ExitStack()
    with ctx:
        place = [SBUF_AT]

        def sb(name, shape, dt=F32):
            at, n = place[0], 2 if dt is BF16 else 4
            for d in shape[1:]:
                n *= d
            place[0] = at + (n + 31) // 32 * 32
            return nc.alloc_sbuf_tensor_at(name, shape, dt, offset=at)

        def sem(name):
            return ctx.enter_context(nc.semaphore(name))

        h = sb("h", [P, NT, D])
        mem_at = place[0]
        mem = sb("mem", [P, 3 * 12288 + 8960])

        def rounded(name, first, n):
            return nc.alloc_sbuf_tensor_at(name, [P, n], F32R, offset=mem_at + 4 * first)

        hi4, lo4 = rounded("hi4", 0, 4096), rounded("lo4", 12288, 4096)
        hi8, lo8 = rounded("hi8", 4096, 8192), rounded("lo8", 24576, 8192)
        raw8 = nc.alloc_sbuf_tensor_at("raw8", [P, 8192], F32, offset=mem_at + 4 * 24576)
        raw4 = nc.alloc_sbuf_tensor_at("raw4", [P, 4096], F32, offset=mem_at + 4 * 12288)

        def tiles(tensor):
            return tensor[:, :].rearrange("p (k t) -> p k t", k=8)

        def chunk_pair(tensor):
            return tensor[:, :].rearrange("p (b k n) -> p b k n", b=2, k=KD)

        xnT, x_hi, x_lo = tiles(raw4), tiles(hi4), tiles(lo4)
        yT, y_hi, y_lo = xnT, x_hi, x_lo
        win, win_hi, win_lo = chunk_pair(raw8), chunk_pair(hi8), chunk_pair(lo8)
        wout, wout_hi, wout_lo = tiles(raw8), tiles(hi8), tiles(lo8)
        wpg_raw = nc.alloc_sbuf_tensor_at("wpg_raw", [P, 8192], F32, offset=mem_at + 4 * 12288)
        wpg, wpg_hi, wpg_lo = tiles(wpg_raw), tiles(hi8), tiles(rounded("wpg_lo", 12288, 8192))
        hp_hi = hi4[:, 0:2048].rearrange("p (b k t) -> p b k t", b=2, k=KD)
        hp_lo = rounded("hp_lo", 24576 + 4096, 2048)[:, :].rearrange("p (b k t) -> p b k t", b=2, k=KD)
        slots = [mem[:, n * 6144:(n + 1) * 6144].rearrange("p (a b) -> p a b", a=3) for n in range(RING)]
        a1 = mem[:, 12288:24576]
        a2 = mem[:, 24576:36864]
        work = mem[:, 36864:]
        u_a, v_a, q_b, k_b = (a1[:, 4096 + 2048 * c:6144 + 2048 * c].rearrange("p (t n) -> p t n", t=NT)
                              for c in range(4))
        ysq = a1[:, 6144:8192].rearrange("p (j t) -> p j t", j=4)
        kT = a2[:, 8192:10240].rearrange("p (j t) -> p j t", j=4)
        v_b = a2[:, 10240:12288].rearrange("p (t n) -> p t n", t=NT)
        wple = a2[:, 8192:10240].rearrange("p (k n) -> p k n", k=2)
        chunks = (u_a, v_a, q_b, k_b, v_b)
        qTz = work[:, 0:4096].rearrange("p (h t) -> p h t", h=H)
        hnT = work[:, 0:4096].rearrange("p (k t) -> p k t", k=KD)
        pW = work[:, 0:4096].rearrange("p (t n) -> p t n", t=NT)
        p_sb = work[:, 4096:5120].rearrange("p (t n) -> p t n", t=NT)
        probs = work[:, 4096:6144].rearrange("p (i k) -> p i k", i=NT)
        PT = work[:, 6144:8704].rearrange("p (b c q) -> p b c q", b=2, c=10)
        xs = work[:, 6144:8192].rearrange("p (b d) -> p b d", b=2)
        junk = work[:, 5120:6144]
        sqs = work[:, 4096:4608]
        wsb = work[:, 8192:8704].rearrange("p (g s) -> p g s", g=GA)
        xg = work[:, 4096:5120]
        xgT = work[:, 5120:6144].rearrange("p (k s) -> p k s", k=KD)
        ysb = work[:, 6144:7168]
        sil = work[:, 8192:8448].rearrange("p (b f) -> p b f", b=2)
        act = work[:, 8448:8704].rearrange("p (b f) -> p b f", b=2)
        aT = work[:, 8704:8960].rearrange("p (b f) -> p b f", b=2)
        yg = [a2[:, b * 2048:(b + 1) * 2048].rearrange("p (k d) -> p k d", k=2) for b in range(2)]
        hpT = a2[:, 4096:6144].rearrange("p (b k t) -> p b k t", b=2, k=KD)
        sg = a2[:, 6144:7168].rearrange("p (b n) -> p b n", b=2)
        gva = sb("gva", [P, DA])
        pT = sb("pT", [P, 2, S])
        wsT = pT[:, 0].rearrange("p (g t) -> p g t", g=GA)

        ident = sb("ident", [P, P])
        causal = sb("causal", [P, P])
        earlier = sb("earlier", [P, P], BF16)
        ones_b = sb("ones_b", [P, P], BF16)
        ones1 = sb("ones1", [P, 1])
        g3 = sb("g3", [P, 3, KD])
        gqk = sb("gqk", [P, 2])
        goab = sb("goab", [P, 8])
        bs = sb("bs", [P, GA])
        wr = sb("wr", [P, KD, NG + E])
        ss3 = sb("ss3", [P, 3, NT])
        rs = sb("rs", [P, 3, NT])
        ssn = sb("ssn", [P, 3, 32])
        rsn = sb("rsn", [P, 3, 32])
        ssab = sb("ssab", [P, 2, NT])
        rsab = sb("rsab", [P, 2, NT])
        rt = sb("rt", [P, 32])
        nmx = sb("nmx", [P, H * NT])
        rsum = sb("rsum", [P, H * NT])
        rrec = sb("rrec", [P, H * NT])
        scratch = work[:, 5120:8960]
        used = [0]

        def tmp(*shape, rows=P, dt=F32):
            n, at = 1, used[0]
            for d in shape:
                n *= d
            used[0] += n
            assert used[0] <= 3840
            v = scratch[0:rows, at:at + n]
            if dt is not F32:
                v = v.bitcast(dt)
            names = "abc"[:len(shape)]
            return v.rearrange(f"p ({' '.join(names)}) -> p {' '.join(names)}", **dict(zip(names, shape)))

        lgT = tmp(S, rows=NG + E)
        lg = tmp(NT, NG + E)
        r4 = tmp(NT, 4)
        oh_g = tmp(NT, NG)
        r32 = tmp(NT, E)
        s32 = tmp(NT, E)
        r8 = tmp(NT, EPG)
        t8 = tmp(NT, EPG)
        oh1 = tmp(NT, EPG)
        oh2 = tmp(NT, EPG)
        m12 = tmp(4, NT)
        M1 = tmp(NT, E)
        M2 = tmp(NT, E)
        cnt = tmp(E)
        cmp8 = tmp(E, EPG)
        chunks_of = tmp(E)
        nr = tmp(NPAIR)
        incl = tmp(NPAIR)
        base = tmp(NPAIR)
        z0 = tmp(E)
        Ri = tmp(NT, E, dt=I32)
        Fi = tmp(NT, E, dt=I32)
        posf = tmp(2, NT)
        posi = tmp(2, NT, dt=I32)
        rndi = tmp(2, NT, dt=I32)
        rowf = tmp(2 * NT)
        rndf = tmp(2 * NT)
        ohs = tmp(2 * NT, P)
        ohb = tmp(2 * NT, NR)
        tbl = tmp(NR)
        tb2 = tmp(NR)
        none = tmp(NR)
        regf = tmp(4 * NPAIR + 1)
        Mb = sb("Mb", [P, NT, E], BF16)
        cw = sb("cw", [P, 2, NT])
        gidx = sb("gidx", [P, NR], U32)
        sidx = sb("sidx", [P, NR], U32)
        gcol = sb("gcol", [P, 1], U32)
        scol = sb("scol", [P, 1], U32)
        regs = sb("regs", [P, 4 * NPAIR + 1], I32)
        rowv = sb("rowv", [P, 2, NT])
        n64 = sb("n64", [P, EPG])
        odd64 = sb("odd64", [P, NPAIR, 2])
        first = sb("first", [P, EPG])
        slf = sb("slf", [P, P])

        ps = [ctx.enter_context(nc.psum_tensor(f"ps{i}", [P, 512], F32)) for i in range(8)]

        ld_x = [sem(f"ld_x{t}") for t in range(NT)]
        ld_gain = sem("ld_gain")
        ld_small = sem("ld_small")
        ld_win = [sem(f"ld_win{b}") for b in range(2)]
        ld_win0 = [sem(f"ld_win0_{c}") for c in range(4)]
        ld_wout = [sem(f"ld_wout{b}") for b in range(2)]
        ld_ple = sem("ld_ple")
        ld_gu = [sem(f"ld_gu{b}") for b in range(RING)]
        ld_down = [sem(f"ld_down{b}") for b in range(RING)]
        ld_wpg = [sem(f"ld_wpg{b}") for b in range(2)]
        ld_xg = sem("ld_xg")
        ld_yg = [sem(f"ld_yg{b}") for b in range(2)]
        st_hn = [sem(f"st_hn{b}") for b in range(2)]
        st_y = sem("st_y")
        st_out = sem("st_out")
        consts = sem("consts")
        sq_done = [sem(f"sq_done{k}") for k in range(3)]
        xs_ready = [sem(f"xs_ready{k}") for k in range(3)]
        xt_done = [sem(f"xt_done{k}") for k in range(3)]
        nT_ready = [sem(f"nT_ready{k}") for k in range(3)]
        xhi_ready = sem("xhi_ready")
        xlo_ready = sem("xlo_ready")
        whi_ready = sem("whi_ready")
        wlo_ready = sem("wlo_ready")
        ws_done = sem("ws_done")
        ws_ready = sem("ws_ready")
        proj_done = sem("proj_done")
        proj_ev = sem("proj_ev")
        qk_ready = sem("qk_ready")
        v_ready = sem("v_ready")
        gq_ready = sem("gq_ready")
        kt_done = sem("kt_done")
        kt_ready = sem("kt_ready")
        qt_done = sem("qt_done")
        qt_ready = [sem(f"qt_ready{b}") for b in range(2)]
        qz_zero = sem("qz_zero")
        mix_done = sem("mix_done")
        ya_ready = sem("ya_ready")
        sa_done = sem("sa_done")
        rsab_ready = sem("rsab_ready")
        ya_scaled = sem("ya_scaled")
        yat_done = sem("yat_done")
        yat_ready = sem("yat_ready")
        s_done = sem("s_done")
        nmx_ready = sem("nmx_ready")
        exp_done = sem("exp_done")
        p_ready = sem("p_ready")
        pt_done = sem("pt_done")
        pt_ready = sem("pt_ready")
        pv_done = sem("pv_done")
        yb_ready = sem("yb_ready")
        ysq_ready = sem("ysq_ready")
        sb_done = sem("sb_done")
        sb_read = sem("sb_read")
        wohi_ready = sem("wohi_ready")
        wolo_ready = sem("wolo_ready")
        yahi_ready = sem("yahi_ready")
        yalo_ready = sem("yalo_ready")
        ybhi_ready = sem("ybhi_ready")
        yblo_ready = sem("yblo_ready")
        wo_done = sem("wo_done")
        h_ready = sem("h_ready")
        lgt_done = sem("lgt_done")
        lgt_ready = sem("lgt_ready")
        lg_done = sem("lg_done")
        ex_in = sem("ex_in")
        ex_out = sem("ex_out")
        mb_ready = sem("mb_ready")
        rank_done = sem("rank_done")
        oh_ready = sem("oh_ready")
        idx_done = sem("idx_done")
        idx_ready = sem("idx_ready")
        pp_done = sem("pp_done")
        pp_ready = sem("pp_ready")
        pw_done = sem("pw_done")
        pw_ready = sem("pw_ready")
        xgt_done = sem("xgt_done")
        xgt_ready = sem("xgt_ready")
        gu_done = sem("gu_done")
        sil_ready = sem("sil_ready")
        act_ready = sem("act_ready")
        at_done = sem("at_done")
        at_ready = sem("at_ready")
        block_done = sem("block_done")
        ysb_ready = sem("ysb_ready")
        h2_ready = sem("h2_ready")
        pghi_ready = sem("pghi_ready")
        pglo_ready = sem("pglo_ready")
        hphi_ready = sem("hphi_ready")
        hplo_ready = sem("hplo_ready")
        pg_done = sem("pg_done")
        sg_ready = sem("sg_ready")
        sg_used = sem("sg_used")
        out_ready = sem("out_ready")
        dve_step = sem("dve_step")
        pool_step = sem("pool_step")
        column_ready = sem("column_ready")

        ORDER = [2, 3, 1, 4, 0]
        OUT_ORDER = [4, 5, 6, 7, 0, 1, 2, 3]
        block = ctx.enter_context(nc.Block())

        @block.sync
        def _(sp):
            def load_gate(slot, gate):
                sp.dma_start(slots[slot][:, 0], gate).then_inc(ld_gu[slot], 16)

            def load_up(slot, up):
                sp.dma_start(slots[slot][:, 1], up).then_inc(ld_gu[slot], 16)

            def load_down(slot, down):
                for c in range(2):
                    sp.dma_start(slots[slot][:, 2, c * D:c * D + D], down[:, c]).then_inc(ld_down[slot], 16)

            def load_static(e):
                load_gate(e % RING, gate_v[e])
                load_up(e % RING, up_v[e])
                load_down(e % RING, down_v[e])

            def refill(pair, q, e, turn):
                ends = [sp.value_load(regs[0:1, bass.ds(q + (2 + s) * NPAIR, 1)], min_val=3, max_val=2 * NR + 2)
                        for s in range(2)]
                before = (2 * pair - 1) % RING
                turn_before = turn if pair == 0 else turn + 1
                for s in range(2):
                    sp.wait_ge(ld_down[(before + s - 1) % RING], 32 * turn_before)
                    sp.wait_ge(gu_done, ends[s])
                    load_gate(2 * pair + s, gate_v[bass.ds(e + s, 1)].rearrange("a p n -> p (a n)"))
                    load_up(2 * pair + s, up_v[bass.ds(e + s, 1)].rearrange("a p n -> p (a n)"))
                sp.wait_ge(ld_gu[2 * pair], 32 * turn + 32)
                for s in range(2):
                    sp.wait_ge(block_done, ends[s])
                    load_down(2 * pair + s, down_v[bass.ds(e + s, 1)].rearrange("a p c d -> p (a c) d"))

            for t in range(NT):
                sp.dma_start(h[:, t], x_v[t]).then_inc(ld_x[t], 16)
            for c in range(4):
                sp.dma_start(win[:, 0, 2 * c:2 * c + 2], win_v[:, 2 * c:2 * c + 2, ORDER[0] * 512:ORDER[0] * 512 + 512])\
                    .then_inc(ld_win0[c], 16)
            sp.dma_start(win[:, 1], win_v[:, :, ORDER[1] * 512:ORDER[1] * 512 + 512]).then_inc(ld_win[1], 16)
            small = [(wsb, w_s[0].rearrange("g t s -> t g s")),
                     (gva[:, :], g_v_a[0:1, :].broadcast_to([P, DA])),
                     (bs[:, :], b_s[0].rearrange("g t -> t g")),
                     (gqk[0:64, 0:1], g_q[0:1].rearrange("a d -> d a")),
                     (gqk[64:128, 0:1], g_q[0:1].rearrange("a d -> d a")),
                     (gqk[0:64, 1:2], g_k[0:1].rearrange("a d -> d a")),
                     (gqk[64:128, 1:2], g_k[0:1].rearrange("a d -> d a")),
                     (goab[:, 0:4], g_out_a[0].rearrange("(k p) -> p k", p=P)),
                     (goab[:, 4:8], g_out_b[0].rearrange("(k p) -> p k", p=P)),
                     (g3[:, 1], g_ffn[0].rearrange("(p k) -> p k", k=KD)),
                     (g3[:, 2], g_ple[0].rearrange("(p k) -> p k", k=KD)),
                     (wr[:, :, 0:NG], w_group[0].rearrange("(p k) n -> p k n", k=KD)),
                     (wr[:, :, NG:], w_expert[0].rearrange("(p k) n -> p k n", k=KD))]
            assert len(small) == N_SMALL
            for dst, src in small:
                sp.dma_start(dst, src, allow_slow_non_contiguous=True).then_inc(ld_small, 16)
            for n in range(2, 5):
                sp.wait_ge(proj_done, NT * (n - 1))
                sp.dma_start(win[:, n % 2], win_v[:, :, ORDER[n] * 512:ORDER[n] * 512 + 512])\
                    .then_inc(ld_win[n % 2], 16)
            for b, n in ((1, 3), (0, 4)):
                sp.wait_ge(proj_done, NT * (n + 1))
                sp.dma_start(wout[:, 4 * b:4 * b + 4], wout_v[:, 4 * b:4 * b + 4]).then_inc(ld_wout[b], 16)
            sp.wait_ge(qt_done, NT)
            load_up(3, up_v[3])
            load_down(3, down_v[3])
            sp.wait_ge(pv_done, H)
            sp.dma_start(wple, wple_v).then_inc(ld_ple, 16)
            sp.dma_start(p_sb, p_v).then_inc(ld_ple, 16)
            load_down(5, down_v[5])
            sp.wait_ge(sb_done, 1)
            load_gate(3, gate_v[3])
            def store_rows(t):
                sp.wait_ge(xs_ready[1], t + 1)
                sp.dma_start(hn_dram[t * P:t * P + P], xs[:, t % 2]).then_inc(st_hn[t % 2], 16)

            for t in range(NT - 1):
                store_rows(t)
            sp.wait_ge(wo_done, 2 * NT)
            load_gate(0, gate_v[0])
            load_up(0, up_v[0])
            store_rows(NT - 1)
            load_down(0, down_v[0])
            load_static(1)
            load_static(2)
            load_static(4)
            load_gate(5, gate_v[5])
            sp.wait_ge(ld_xg, 16)
            sp.wait_ge(pw_done, 2 * NT)
            load_up(5, up_v[5])
            sp.wait_ge(idx_ready, 1)
            with sp.Fori(0, NPAIR // 3 - 1) as i:
                for pair in range(3):
                    refill(pair, 3 * i + pair, 6 * i + (6 + 2 * pair), i + 1)
            refill(0, NPAIR - 4, E - 2, NPAIR // 3)
            end = sp.value_load(regs[0:1, 4 * NPAIR - 3:4 * NPAIR - 2], min_val=3, max_val=2 * NR + 2)
            sp.wait_ge(block_done, end)
            wpg_kn = wpg_v.rearrange("p (k n) -> p k n", k=KD)
            sp.dma_start(wpg[:, :, 0:512], wpg_kn[:, :, 0:512]).then_inc(ld_wpg[0], 16)
            rounds = sp.value_load(regs[0:1, 4 * NPAIR:4 * NPAIR + 1], min_val=NPAIR, max_val=NR - 1)
            sp.wait_ge(st_y, 16 * rounds)
            for t in range(NT):
                if t == 2:
                    sp.dma_start(wpg[:, :, 512:], wpg_kn[:, :, 512:]).then_inc(ld_wpg[1], 16)
                if t >= 2:
                    sp.wait_ge(h2_ready, 2 * (t - 1))
                sp.dma_start(yg[t % 2], y_v[t]).then_inc(ld_yg[t % 2], 16)
            for t in range(NT):
                sp.wait_ge(out_ready, t + 1)
                sp.dma_start(out_v[t], h[:, t]).then_inc(st_out, 16)
            sp.wait_ge(st_out, 16 * NT)

        @block.gpsimd
        def _(pool):
            steps = [0]

            def link(ins):
                steps[0] += 1
                ins.then_inc(pool_step, 1)
                pool.wait_ge(pool_step, steps[0])

            link(pool.memset(ident[:, :], 0.0))
            link(pool.affine_select(out=ident[:, :], in_=ident[:, :], compare_op=ALU.not_equal, fill=1.0, base=0,
                                    pattern=[[-1, P]], channel_multiplier=1))
            link(pool.memset(causal[:, :], 0.0))
            link(pool.affine_select(out=causal[:, :], in_=causal[:, :], compare_op=ALU.is_ge, fill=NEG, base=0,
                                    pattern=[[-1, P]], channel_multiplier=1))
            link(pool.memset(ones_b[:, :], 1.0))
            link(pool.affine_select(out=earlier[:, :], in_=ones_b[:, :], compare_op=ALU.is_gt, fill=0.0, base=0,
                                    pattern=[[1, P]], channel_multiplier=-1))
            for dst, pattern, first_value, mult in ((rowv, [[S, 2], [P, NT]], 1, 1), (n64, [[BLK, EPG]], 0, 0),
                                                    (odd64, [[0, NPAIR], [BLK, 2]], 0, 0),
                                                    (first, [[-1, EPG]], EPG, 0), (slf, [[1, P]], 0, 0)):
                link(pool.iota(dst[:], pattern=pattern, base=first_value, channel_multiplier=mult,
                               allow_small_or_imprecise_dtypes=True))
            pool.memset(ones1[:, :], 1.0).then_inc(consts, 1)
            pool.wait_ge(ws_ready, 1)
            pool.affine_select(out=wsT, in_=wsT, compare_op=ALU.is_ge, fill=0.0, base=0,
                               pattern=[[0, GA], [1, P]], channel_multiplier=-1).then_inc(ws_ready, 1)
            pool.wait_ge(ws_ready, 2)
            pool.memset(qTz[64:128].rearrange("p (j b) t -> p j b t", b=2)[:, :, 0], 0.0).then_inc(qz_zero, 1)
            pool.wait_ge(qz_zero, 1)
            pool.memset(qTz[0:64].rearrange("p (j b) t -> p j b t", b=2)[:, :, 1], 0.0).then_inc(qz_zero, 1)
            for n, k in enumerate(OUT_ORDER):
                pool.wait_ge(wohi_ready, n + 1)
                pool.tensor_tensor(wout_lo[:, k], wout[:, k], wout_hi[:, k], ALU.subtract).then_inc(wolo_ready, 1)
                if n == 3:
                    pool.wait_ge(rsab_ready, 1)
                    for t in range(NT):
                        pool.tensor_scalar(u_a[:, t], u_a[:, t], rsab[:, 0, t:t + 1], None, ALU.mult)\
                            .then_inc(ya_scaled, 1)
            pool.wait_ge(idx_ready, 1)
            for b in range(2):
                pool.wait_ge(st_hn[b], 32)
            rounds = pool.value_load(regs[0:1, 4 * NPAIR:4 * NPAIR + 1], min_val=NPAIR, max_val=NR - 1)
            pool.indirect_dma_start(out=xg, out_offset=None, in_=hn_dram,
                                    in_offset=bass.IndirectOffsetOnAxis(ap=gidx[:, 0:1], axis=0),
                                    bounds_check=S - 1, oob_is_err=False).then_inc(ld_xg, 16)
            pool.wait_ge(xgt_done, 2)
            pool.indirect_dma_start(out=xg, out_offset=None, in_=hn_dram,
                                    in_offset=bass.IndirectOffsetOnAxis(ap=gidx[:, 1:2], axis=0),
                                    bounds_check=S - 1, oob_is_err=False).then_inc(ld_xg, 16)

            def gather(r):
                pool.wait_ge(xgt_done, 2 * r)
                pool.tensor_copy(gcol[:, :], gidx[:, bass.ds(r, 1)]).then_inc(column_ready, 1)
                pool.wait_ge(column_ready, 1)
                pool.sem_clear(column_ready)
                pool.indirect_dma_start(out=xg, out_offset=None, in_=hn_dram,
                                        in_offset=bass.IndirectOffsetOnAxis(ap=gcol[:, :], axis=0),
                                        bounds_check=S - 1, oob_is_err=False)\
                    .then_inc(ld_xg, 16)

            def scatter(r):
                pool.wait_ge(ysb_ready, 2 * r + 4)
                pool.tensor_copy(scol[:, :], sidx[:, bass.ds(r, 1)]).then_inc(column_ready, 1)
                pool.wait_ge(column_ready, 1)
                pool.sem_clear(column_ready)
                pool.indirect_dma_start(out=y_dram, out_offset=bass.IndirectOffsetOnAxis(ap=scol[:, :], axis=0),
                                        in_=ysb, in_offset=None, bounds_check=PAIRS - 1, oob_is_err=False)\
                    .then_inc(st_y, 16)

            with pool.Fori(0, rounds - 1) as r:
                gather(r + 2)
                scatter(r)
            scatter(rounds - 1)

        @block.tensor
        def _(pe):
            mm = nc.tensor.matmul

            def transposes_of_tile(k, t, bank=None):
                pe.wait_ge(xs_ready[k], t + 1)
                back = 2 if k == 0 else 1
                if t >= back:
                    pe.wait_ge(nT_ready[k], t - back + 1)
                rows = xs[:, t % 2].rearrange("p (a k) -> p k a", k=KD)
                bank = 2 * (t % 2) if k == 0 else 4
                for j in range(KD):
                    last = nc.tensor.transpose(ps[bank + j // 4][:, j % 4 * P:j % 4 * P + P], rows[:, j], ident[:, :])
                last.then_inc(xt_done[k], 1)

            pe.wait_ge(consts, 1)

            def project(n, t):
                m = n * NT + t
                if n == 0:
                    pe.wait_ge(xhi_ready, t + 1)
                    pe.wait_ge(xlo_ready, t + 1)
                if m >= 2:
                    pe.wait_ge(proj_ev, m - 1)
                for k in range(KD):
                    if t == 0 and k % 2 == 0:
                        pe.wait_ge(whi_ready, 4 * n + k // 2 + 1)
                        pe.wait_ge(wlo_ready, 4 * n + k // 2 + 1)
                    for a, b in ((x_hi, win_hi), (x_hi, win_lo), (x_lo, win_hi)):
                        last = mm(ps[4 + m % 2][:, :], a[:, k, t * P:t * P + P], b[:, n % 2, k],
                                  start=(k == 0 and a is x_hi and b is win_hi), stop=(k == KD - 1 and a is x_lo))
                last.then_inc(proj_done, 1)

            transposes_of_tile(0, 0)
            for t in range(NT):
                if t + 1 < NT:
                    transposes_of_tile(0, t + 1)
                project(0, t)
            pe.wait_ge(ld_small, 16 * N_SMALL)
            for g in range(GA):
                last = nc.tensor.transpose(ps[6][:, g * P:g * P + P], wsb[:, g], ident[:, :])
            last.then_inc(ws_done, 1)
            for n in range(1, 5):
                for t in range(NT):
                    project(n, t)
                    if n == 3:
                        pe.wait_ge(qk_ready, NT + t + 1)
                        if t >= 2:
                            pe.wait_ge(kt_ready, t - 1)
                        for j in range(4):
                            last = nc.tensor.transpose(ps[t % 2][:, j * P:j * P + P], k_b[:, t, j * P:j * P + P],
                                                       ident[:, :])
                        last.then_inc(kt_done, 1)
            pe.wait_ge(kt_ready, NT)
            pe.wait_ge(qz_zero, 2)
            for t in range(NT):
                for j in range(4):
                    last = nc.tensor.transpose(ps[t][:, j * P:j * P + P], q_b[:, t, j * P:j * P + P], ident[:, :])
                last.then_inc(qt_done, 1)
            def scores(hh, i):
                n = hh * NT + i
                if hh:
                    pe.wait_ge(exp_done, n - NT + 1)
                mm(ps[i][:, 0:(i + 1) * P], qTz[:, hh, i * P:i * P + P], kT[:, hh // 2, 0:(i + 1) * P],
                   start=True, stop=True).then_inc(s_done, 1)

            for b in range(2):
                pe.wait_ge(qt_ready[b], NT)
            pe.wait_ge(proj_ev, 5 * NT)
            for i in range(NT):
                scores(0, i)
            pe.wait_ge(ws_ready, 2)
            pe.wait_ge(v_ready, NT)
            for g in range(GA):
                if g >= 2:
                    pe.wait_ge(ya_ready, g - 1)
                mm(ps[6 + g % 2][:, :], wsT[:, g], v_a[:, :, g * P:g * P + P], start=True, stop=True)\
                    .then_inc(mix_done, 1)


            def values(hh):
                pe.wait_ge(pt_ready, NT * (hh + 1))
                if hh % 2 == 0:
                    if hh >= 4:
                        pe.wait_ge(yb_ready, hh // 2 - 1)
                        pe.wait_ge(ysq_ready, hh // 2 - 1)
                    else:
                        pe.wait_ge(ya_ready, GA)
                rows = slice(64 * (hh % 2), 64 * (hh % 2) + 64)
                for i in range(NT):
                    for kt in range(i + 1):
                        last = mm(ps[6 + hh // 2 % 2][rows, i * P:i * P + P], v_b[:, kt, hh * DH:hh * DH + DH],
                                  PT[:, hh % 2, i * (i + 1) // 2 + kt], start=(kt == 0), stop=(kt == i))
                last.then_inc(pv_done, 1)

            for hh in range(H):
                for i in range(NT):
                    n = hh * NT + i
                    if hh + 1 < H:
                        scores(hh + 1, i)
                    pe.wait_ge(p_ready, n + 1)
                    if n >= 2:
                        pe.wait_ge(pt_ready, n - 1)
                    for kt in range(i + 1):
                        last = nc.tensor.transpose(ps[4 + n % 2][:, kt * P:kt * P + P], probs[:, i, kt * P:kt * P + P],
                                                   ident[:, :])
                    last.then_inc(pt_done, 1)
                    if hh and i == 1:
                        values(hh - 1)
            pe.wait_ge(pt_ready, H * NT)
            for t in range(NT):
                pe.wait_ge(ya_scaled, t + 1)
                if t >= 2:
                    pe.wait_ge(yat_ready, t - 1)
                for j in range(4):
                    last = nc.tensor.transpose(ps[4 + t % 2][:, j * P:j * P + P], u_a[:, t, j * P:j * P + P], ident[:, :])
                last.then_inc(yat_done, 1)
                if t == 1:
                    values(H - 1)

            def squares_of_y_b():
                pe.wait_ge(ysq_ready, 4)
                for t in range(NT):
                    for j in range(4):
                        last = mm(ps[6][:, t:t + 1], ysq[:, j, t * P:t * P + P], ones1[:, :],
                                  start=(j == 0), stop=(j == 3))
                last.then_inc(sb_done, 1)

            pe.wait_ge(wohi_ready, 8)
            pe.wait_ge(wolo_ready, 8)
            pe.wait_ge(exp_done, H * NT)

            def output_rows(t):
                for half in range(2):
                    n = 2 * t + half
                    if n >= 2:
                        pe.wait_ge(h_ready, n - 1)
                    if half == 0:
                        pe.wait_ge(yahi_ready, t + 1)
                        pe.wait_ge(yalo_ready, t + 1)
                    for w in range(2):
                        if n == 0 and w == 1:
                            pe.wait_ge(ybhi_ready, 4)
                            pe.wait_ge(yblo_ready, 4)
                        for k in range(4 * w, 4 * w + 4):
                            for a, b in ((y_hi, wout_hi), (y_hi, wout_lo), (y_lo, wout_hi)):
                                last = mm(ps[2 * (n % 2) + w][:, :], a[:, k, t * P:t * P + P],
                                          b[:, k, half * 512:half * 512 + 512],
                                          start=(k == 4 * w and a is y_hi and b is wout_hi),
                                          stop=(k == 4 * w + 3 and a is y_lo))
                    last.then_inc(wo_done, 1)
                    if n == 0:
                        squares_of_y_b()

            def transposes_of_p(t):
                if t == 0:
                    pe.wait_ge(ld_ple, 32)
                else:
                    pe.wait_ge(pp_ready, t)
                for k in range(2):
                    last = nc.tensor.transpose(ps[7][:, k * P:k * P + P], p_sb[:, t, k * P:k * P + P], ident[:, :])
                last.then_inc(pp_done, 1)

            for t in range(NT):
                output_rows(t)
                if t:
                    transposes_of_tile(1, t - 1)
                transposes_of_p(t)
            def embedding(t):
                pe.wait_ge(pp_ready, t + 1)
                for half in range(2):
                    n = 2 * t + half
                    if n >= 2:
                        pe.wait_ge(pw_ready, n - 1)
                    for k in range(2):
                        last = mm(ps[n % 2][:, :], pT[:, k, t * P:t * P + P], wple[:, k, half * 512:half * 512 + 512],
                                  start=(k == 0), stop=(k == 1))
                    last.then_inc(pw_done, 1)

            transposes_of_tile(1, NT - 1)
            pe.wait_ge(nT_ready[1], NT)
            pe.wait_ge(sb_read, 1)
            for k in range(KD):
                last = mm(ps[6][0:NG + E, :], wr[:, k], hnT[:, k], start=(k == 0), stop=(k == KD - 1))
            last.then_inc(lgt_done, 1)
            pe.wait_ge(lgt_ready, 1)
            for t in range(NT):
                last = nc.tensor.transpose(ps[4][:, t * (NG + E):(t + 1) * (NG + E)], lgT[:, t * P:t * P + P],
                                           ident[0:NG + E, 0:NG + E])
            last.then_inc(lg_done, 1)
            pe.wait_ge(h_ready, 2 * NT)
            embedding(0)
            pe.wait_ge(mb_ready, 1)
            for t in range(NT):
                for t2 in range(t + 1):
                    mm(ps[5][:, t * E:t * E + E], (earlier if t2 == t else ones_b)[:, :], Mb[:, t2],
                       start=(t2 == 0), stop=(t2 == t))
            for t2 in range(NT):
                last = mm(ps[5][:, NT * E:NT * E + E], ones_b[:, :], Mb[:, t2], start=(t2 == 0), stop=(t2 == NT - 1))
            last.then_inc(rank_done, 1)
            embedding(1)
            embedding(2)
            pe.wait_ge(oh_ready, 1)
            for n in range(2 * NT):
                last = mm(ps[6][:, 0:NR], ohs[:, n], ohb[:, n],
                          start=(n == 0), stop=(n == 2 * NT - 1))
            last.then_inc(idx_done, 1)
            embedding(3)
            pe.wait_ge(idx_ready, 1)

            def transpose_half(half, n):
                rows = xg.rearrange("p (a k) -> p k a", k=KD)
                pe.wait_ge(ld_xg, n)
                for k in range(4):
                    last = nc.tensor.transpose(ps[6 + half][:, k * P:k * P + P], rows[:, 4 * half + k], ident[:, :])
                last.then_inc(xgt_done, 1)

            def expert_round(n, pair, loaded):
                pe.wait_ge(xgt_ready, n + 2)
                for s in range(2):
                    w = slots[2 * pair + s]
                    pe.wait_ge(ld_gu[2 * pair + s], 32 * loaded)
                    pe.wait_ge(act_ready, n + (s + 1))
                    for k in range(KD):
                        for c in range(2):
                            last = mm(ps[s][64 * c:64 * c + 64, 0:256], xgT[:, k, s * BLK:s * BLK + BLK],
                                      w[:, 0:2, k * FF + c * P:k * FF + c * P + P], start=(k == 0), stop=(k == KD - 1))
                    last.then_inc(gu_done, 1)
                for s in range(2):
                    w = slots[2 * pair + s]
                    pe.wait_ge(act_ready, n + (s + 3))
                    nc.tensor.transpose(ps[4][:, s * P:s * P + P], act[:, s], ident[:, :]).then_inc(at_done, 1)
                    transpose_half(s, 8 * n + 32)
                    pe.wait_ge(ld_down[2 * pair + s], 32 * loaded)
                    pe.wait_ge(at_ready, n + (s + 1))
                    pe.wait_ge(ysb_ready, n + (s + 1))
                    for c in range(2):
                        for half in range(2):
                            last = mm(ps[2 + s][64 * half:64 * half + 64, :], aT[:, s, c * 64:c * 64 + 64],
                                      w[:, 2, c * D + half * 512:c * D + half * 512 + 512],
                                      start=(c == 0), stop=(c == 1))
                    last.then_inc(block_done, 1)

            def pair_rounds(q, pair, loaded):
                rounds = pe.value_load(regs[0:1, bass.ds(q, 1)], min_val=1, max_val=S // BLK)
                before = pe.value_load(regs[0:1, bass.ds(q + NPAIR, 1)], min_val=0, max_val=2 * NR)
                with pe.Fori(0, rounds) as k:
                    expert_round(before + 2 * k, pair, loaded)

            pe.sem_inc(gu_done, 2)
            pe.sem_inc(at_done, 2)
            pe.sem_inc(block_done, 2)
            pe.wait_ge(pw_ready, 2 * NT)
            for half in range(2):
                transpose_half(half, 16)
            with pe.Fori(0, NPAIR // 3) as i:
                for s in range(3):
                    pair_rounds(3 * i + s, s, i + 1)
            pair_rounds(NPAIR - 1, 0, NPAIR // 3 + 1)
            transposes_of_tile(2, 0)
            for t in range(NT):
                for half in range(2):
                    n = 2 * t + half
                    if half == 0:
                        pe.wait_ge(hphi_ready, t + 1)
                        pe.wait_ge(hplo_ready, t + 1)
                    if n >= 4:
                        pe.wait_ge(sg_ready, n - 3)
                    for k in range(KD):
                        if t == 0 and k % 2 == 0:
                            pe.wait_ge(pghi_ready, 4 * half + k // 2 + 1)
                            pe.wait_ge(pglo_ready, 4 * half + k // 2 + 1)
                        for a, b in ((hp_hi, wpg_hi), (hp_hi, wpg_lo), (hp_lo, wpg_hi)):
                            last = mm(ps[n % 4][:, :], a[:, t % 2, k], b[:, k, half * 512:half * 512 + 512],
                                      start=(k == 0 and a is hp_hi and b is wpg_hi), stop=(k == KD - 1 and a is hp_lo))
                    last.then_inc(pg_done, 1)
                    if half == 0 and t + 1 < NT:
                        transposes_of_tile(2, t + 1)

        @block.scalar
        def _(act_e):
            e_ = nc.scalar

            def squares(k, t):
                e_.activation(junk, h[:, t], ACT.Square, accum_out=ss3[:, k, t:t + 1]).then_inc(sq_done[k], 1)
                act_e.wait_ge(sq_done[k], t + 1)

            act_e.dma_start(g3[:, 0], g_mix[0].rearrange("(p k) -> p k", k=KD)).then_inc(ld_gain, 16)
            for t in range(NT):
                act_e.wait_ge(ld_x[t], 16)
                squares(0, t)

            def upper_weights(n):
                if n:
                    act_e.wait_ge(ld_win[n % 2], 16 * ((n + 1) // 2))
                if n >= 2:
                    act_e.wait_ge(proj_done, NT * (n - 1))
                for k in range(0, KD, 2):
                    if n == 0:
                        act_e.wait_ge(ld_win0[k // 2], 16)
                    e_.activation(win_hi[:, n % 2, k:k + 2], win[:, n % 2, k:k + 2], ACT.Copy).then_inc(whi_ready, 1)

            def upper_x(t):
                act_e.wait_ge(nT_ready[0], t + 1)
                e_.activation(x_hi[:, :, t * P:t * P + P], xnT[:, :, t * P:t * P + P], ACT.Copy).then_inc(xhi_ready, 1)

            upper_x(0)
            upper_weights(0)
            for n, c in enumerate(ORDER):
                for t in range(NT):
                    m = n * NT + t
                    if n == 0 and t + 1 < NT:
                        upper_x(t + 1)
                    if t == 2 and n + 1 < len(ORDER):
                        upper_weights(n + 1)
                    act_e.wait_ge(proj_done, m + 1)
                    e_.activation(chunks[c][:, t], ps[4 + m % 2][:, :], ACT.Gelu_apprx_tanh if c < 2 else ACT.Copy)\
                        .then_inc(proj_ev, 1)
            act_e.wait_ge(gq_ready, 1)
            for t in range(NT):
                act_e.wait_ge(qt_done, t + 1)
                e_.activation(qTz[64:128].rearrange("p (j b) t -> p j b t", b=2)[:, :, 1, t * P:t * P + P],
                              ps[t][64:128, :].rearrange("p (j t) -> p j t", j=4), ACT.Copy, scale=gqk[64:128, 0:1])\
                    .then_inc(qt_ready[1], 1)
            def exps(hh, i):
                n = hh * NT + i
                act_e.wait_ge(nmx_ready, n + 1)
                e_.activation(probs[:, i, 0:(i + 1) * P], ps[i][:, 0:(i + 1) * P], ACT.Exp, bias=nmx[:, n:n + 1],
                              accum_out=rsum[:, n:n + 1]).then_inc(exp_done, 1)

            def squares_of_rows(j):
                act_e.wait_ge(yb_ready, j + 1)
                e_.activation(ysq[:, j], ps[6 + j % 2][:, :], ACT.Square).then_inc(ysq_ready, 1)

            def upper_rows(j):
                act_e.wait_ge(yb_ready, j + 1)
                e_.activation(y_hi[:, 4 + j], yT[:, 4 + j], ACT.Copy).then_inc(ybhi_ready, 1)

            for i in range(NT - 1):
                exps(0, i)
            for hh in range(H):
                for i in range(NT):
                    n = hh * NT + i
                    act_e.wait_ge(pt_done, n + 1)
                    if hh >= 2:
                        act_e.wait_ge(pv_done, hh - 1)
                    e_.activation(PT[:, hh % 2, i * (i + 1) // 2:(i + 1) * (i + 2) // 2].rearrange("p a b -> p (a b)"),
                                  ps[4 + n % 2][:, 0:(i + 1) * P], ACT.Copy).then_inc(pt_ready, 1)
                    if n + NT - 1 < H * NT:
                        exps((n + NT - 1) // NT, (n + NT - 1) % NT)
                    if i == 1:
                        k = OUT_ORDER[hh]
                        act_e.wait_ge(ld_wout[k // 4], 16)
                        e_.activation(wout_hi[:, k], wout[:, k], ACT.Copy).then_inc(wohi_ready, 1)
                    if hh and hh % 2 == 0 and i == 3:
                        squares_of_rows(hh // 2 - 1)
                        upper_rows(hh // 2 - 1)
                if hh == 0:
                    act_e.wait_ge(ya_ready, GA)
                    for t in range(NT):
                        e_.activation(PT[:, 1, 0:4].rearrange("p c q -> p (c q)"), u_a[:, t], ACT.Square,
                                      accum_out=ssab[:, 0, t:t + 1]).then_inc(sa_done, 1)
                        act_e.wait_ge(sa_done, t + 1)
            for t in range(NT):
                act_e.wait_ge(yat_ready, t + 1)
                c = slice(t * P, t * P + P)
                e_.activation(y_hi[:, 0:4, c], yT[:, 0:4, c], ACT.Copy).then_inc(yahi_ready, 1)
                if t == 1:
                    upper_rows(H // 2 - 1)
            squares_of_rows(H // 2 - 1)
            for t in range(NT):
                act_e.wait_ge(h_ready, 2 * (t + 1))
                if t == 0:
                    act_e.wait_ge(pv_done, H)
                squares(1, t)
                act_e.wait_ge(pp_done, t + 1)
                e_.activation(pT[:, :, t * P:t * P + P], ps[7][:, 0:2 * P].rearrange("p (k t) -> p k t", k=2), ACT.Copy)\
                    .then_inc(pp_ready, 1)
            act_e.wait_ge(lgt_done, 1)
            e_.activation(lgT[:, :], ps[6][0:NG + E, :], ACT.Copy).then_inc(lgt_ready, 1)
            act_e.wait_ge(ex_in, 1)
            e_.activation(lg[:, :, 0:NG], lg[:, :, 0:NG], ACT.Exp).then_inc(ex_out, 1)
            act_e.wait_ge(ex_in, 2)
            e_.activation(m12[:, 2], m12[:, 1], ACT.Exp).then_inc(ex_out, 1)
            for n in range(2 * NT):
                act_e.wait_ge(pw_done, n + 1)
                e_.activation(pW[:, n // 2, n % 2 * 512:n % 2 * 512 + 512], ps[n % 2][:, :], ACT.Copy)\
                    .then_inc(pw_ready, 1)
            act_e.wait_ge(idx_ready, 1)
            rounds = act_e.value_load(regs[0:1, 4 * NPAIR:4 * NPAIR + 1], min_val=NPAIR, max_val=NR - 1)
            act_e.sem_inc(ysb_ready, 2)

            def round_of_blocks(r, first):
                for s in range(2):
                    act_e.wait_ge(gu_done, 2 * r + (s + 3))
                    act_e.wait_ge(act_ready, 2 * r + (s + 1))
                    e_.activation(sil[:, s], ps[s][:, 0:P], ACT.Silu).then_inc(sil_ready, 1)
                for s in range(2):
                    act_e.wait_ge(block_done, 2 * r + (s + 3))
                    if s == 0 and not first:
                        act_e.wait_ge(st_y, 16 * r)
                    for half in range(2):
                        ins = e_.activation(ysb[s * BLK:s * BLK + BLK, half * 512:half * 512 + 512],
                                            ps[2 + s][64 * half:64 * half + 64, :], ACT.Copy)
                    ins.then_inc(ysb_ready, 1)

            round_of_blocks(0, True)
            with act_e.Fori(1, rounds) as r:
                round_of_blocks(r, False)

            def sigmoids(t):
                for half in range(2):
                    n = 2 * t + half
                    act_e.wait_ge(pg_done, n + 1)
                    if n >= 2:
                        act_e.wait_ge(sg_used, n - 1)
                    e_.activation(sg[:, n % 2], ps[n % 4][:, :], ACT.Sigmoid).then_inc(sg_ready, 1)


            def upper_gate(half):
                act_e.wait_ge(ld_wpg[half], 16)
                c = slice(half * 512, half * 512 + 512)
                for k in range(0, KD, 2):
                    e_.activation(wpg_hi[:, k:k + 2, c], wpg[:, k:k + 2, c], ACT.Copy).then_inc(pghi_ready, 1)

            def squares_of_result(t):
                act_e.wait_ge(h2_ready, 2 * (t + 1))
                squares(2, t)

            upper_gate(0)
            squares_of_result(0)
            squares_of_result(1)
            for t in range(NT):
                act_e.wait_ge(nT_ready[2], t + 1)
                if t >= 2:
                    act_e.wait_ge(pg_done, 2 * (t - 1))
                e_.activation(hp_hi[:, t % 2], hpT[:, t % 2], ACT.Copy).then_inc(hphi_ready, 1)
                if t == 0:
                    upper_gate(1)
                if t + 2 < NT:
                    squares_of_result(t + 2)
                if t:
                    sigmoids(t - 1)
            sigmoids(NT - 1)

        @block.vector
        def _(dve):
            v = nc.vector
            steps = [0]

            def link(ins):
                steps[0] += 1
                ins.then_inc(dve_step, 1)
                dve.wait_ge(dve_step, steps[0])

            def rsqrt(dst, m, n, width):
                t = rt[:, 0:width]
                link(v.tensor_scalar(m, m, 1.0 / n, EPS, ALU.mult, ALU.add))
                link(v.tensor_scalar(dst.bitcast(I32), m.bitcast(I32), 1, None, ALU.logical_shift_right))
                link(v.tensor_scalar(dst.bitcast(I32), dst.bitcast(I32), -1.0, MAGIC, ALU.mult, ALU.add))
                for _ in range(3):
                    link(v.tensor_tensor(t, dst, dst, ALU.mult))
                    link(v.scalar_tensor_tensor(out=t, in0=t, scalar=-0.5, in1=m, op0=ALU.mult, op1=ALU.mult))
                    link(v.scalar_tensor_tensor(out=dst, in0=t, scalar=1.5, in1=dst, op0=ALU.add, op1=ALU.mult))

            def scaled_rows(k, t):
                dve.wait_ge(sq_done[k], t + 1)
                rsqrt(rs[:, k, t:t + 1], ss3[:, k, t:t + 1], D, 1)
                if t >= 2:
                    dve.wait_ge(xt_done[k], t - 1)
                    if k == 1:
                        dve.wait_ge(st_hn[t % 2], 16)
                v.tensor_scalar(xs[:, t % 2], h[:, t], rs[:, k, t:t + 1], None, ALU.mult).then_inc(xs_ready[k], 1)

            def normed(k, t, dst):
                dve.wait_ge(xt_done[k], t + 1)
                bank = 2 * (t % 2) if k == 0 else 4
                for b in range(2):
                    ins = v.tensor_tensor(dst[:, 4 * b:4 * b + 4],
                                          ps[bank + b][:, :].rearrange("p (k t) -> p k t", k=4),
                                          g3[:, k, 4 * b:4 * b + 4].unsqueeze(2).broadcast_to([P, 4, P]), ALU.mult)
                ins.then_inc(nT_ready[k], 1)

            def lower_x(t):
                dve.wait_ge(xhi_ready, t + 1)
                c = slice(t * P, t * P + P)
                v.tensor_tensor(x_lo[:, :, c], xnT[:, :, c], x_hi[:, :, c], ALU.subtract).then_inc(xlo_ready, 1)

            def lower_weights(n):
                for k in range(0, KD, 2):
                    dve.wait_ge(whi_ready, 4 * n + k // 2 + 1)
                    v.tensor_tensor(win_lo[:, n % 2, k:k + 2], win[:, n % 2, k:k + 2], win_hi[:, n % 2, k:k + 2],
                                    ALU.subtract).then_inc(wlo_ready, 1)

            dve.sem_inc(act_ready, 2)
            dve.wait_ge(ld_gain, 16)
            scaled_rows(0, 0)
            scaled_rows(0, 1)
            for t in range(NT):
                if t >= 2:
                    scaled_rows(0, t)
                normed(0, t, xnT[:, :, t * P:t * P + P])
                lower_x(t)
                if t == 0:
                    lower_weights(0)
            lower_weights(1)
            dve.wait_ge(ws_done, 1)
            v.tensor_copy(wsT.rearrange("p g t -> p (g t)"), ps[6][:, :]).then_inc(ws_ready, 1)
            for n, c in enumerate(ORDER[0:3]):
                w = DH if n < 2 else P
                m = DA // w
                for t in range(NT):
                    dve.wait_ge(proj_ev, n * NT + t + 1)
                    link(v.tensor_tensor(sqs, chunks[c][:, t], chunks[c][:, t], ALU.mult))
                    link(v.tensor_reduce(ssn[:, n, t * m:t * m + m], sqs.rearrange("p (a b) -> p a b", b=w),
                                         axis=AX.X, op=ALU.add))
                    if t == 1 and n:
                        lower_weights(n + 1)
                rsqrt(rsn[:, n, 0:NT * m], ssn[:, n, 0:NT * m], w, NT * m)
                for t in range(NT):
                    a = chunks[c][:, t].rearrange("p (a b) -> p a b", b=w)
                    ins = v.tensor_tensor(a, a, rsn[:, n, t * m:t * m + m].unsqueeze(2).broadcast_to([P, m, w]), ALU.mult)
                    if n < 2:
                        ins.then_inc(qk_ready, 1)
                    else:
                        link(ins)
                        v.tensor_tensor(v_a[:, t], v_a[:, t], gva[:, :], ALU.mult).then_inc(v_ready, 1)
            for t in range(NT):
                dve.wait_ge(kt_done, t + 1)
                v.tensor_scalar(kT[:, :, t * P:t * P + P], ps[t % 2][:, :].rearrange("p (j t) -> p j t", j=4),
                                gqk[:, 1:2], None, ALU.mult).then_inc(kt_ready, 1)
                if t == 1:
                    lower_weights(4)
            v.tensor_scalar(gqk[:, 0:1], gqk[:, 0:1], DH ** -0.5, None, ALU.mult).then_inc(gq_ready, 1)
            dve.wait_ge(gq_ready, 1)
            for t in range(NT):
                dve.wait_ge(qt_done, t + 1)
                v.tensor_scalar(qTz[0:64].rearrange("p (j b) t -> p j b t", b=2)[:, :, 0, t * P:t * P + P],
                                ps[t][0:64, :].rearrange("p (j t) -> p j t", j=4), gqk[0:64, 0:1], None, ALU.mult)\
                    .then_inc(qt_ready[0], 1)
            def row_max(hh, i):
                n = hh * NT + i
                dve.wait_ge(s_done, n + 1)
                diag = ps[i][:, i * P:i * P + P]
                link(v.tensor_tensor(diag, diag, causal[:, :], ALU.add))
                v.tensor_reduce(nmx[:, n:n + 1], ps[i][:, 0:(i + 1) * P], axis=AX.X, op=ALU.max, negate=True)\
                    .then_inc(nmx_ready, 1)

            for i in range(NT):
                row_max(0, i)
            dve.wait_ge(proj_ev, 5 * NT)
            for g in range(GA):
                dve.wait_ge(mix_done, g + 1)
                u = u_a[:, :, g * P:g * P + P]
                v.scalar_tensor_tensor(out=u, in0=ps[6 + g % 2][:, :].rearrange("p (n d) -> p n d", n=NT),
                                       scalar=bs[:, g:g + 1], in1=u, op0=ALU.add, op1=ALU.mult).then_inc(ya_ready, 1)

            def scale_probs(n):
                dve.wait_ge(exp_done, n + 1)
                link(v.reciprocal(rrec[:, n:n + 1], rsum[:, n:n + 1]))
                cols = probs[:, n % NT, 0:(n % NT + 1) * P]
                v.tensor_scalar(cols, cols, rrec[:, n:n + 1], None, ALU.mult).then_inc(p_ready, 1)

            def y_b_rows(j):
                dve.wait_ge(pv_done, 2 * j + 2)
                v.tensor_scalar(yT[:, 4 + j], ps[6 + j % 2][:, :], goab[:, 4 + j:5 + j], None, ALU.mult)\
                    .then_inc(yb_ready, 1)

            def lower_rows(j):
                dve.wait_ge(ybhi_ready, j + 1)
                v.tensor_tensor(y_lo[:, 4 + j], yT[:, 4 + j], y_hi[:, 4 + j], ALU.subtract).then_inc(yblo_ready, 1)

            scale_probs(0)
            for hh in range(H):
                for i in range(NT):
                    n = hh * NT + i
                    if n + 1 < H * NT:
                        scale_probs(n + 1)
                    if hh + 1 < H:
                        row_max(hh + 1, i)
                    if hh and hh % 2 == 0 and i == 2:
                        y_b_rows(hh // 2 - 1)
                    if hh >= 3 and hh % 2 and i == 2:
                        lower_rows((hh - 3) // 2)
                if hh == 1:
                    dve.wait_ge(sa_done, NT)
                    rsqrt(rsab[:, 0], ssab[:, 0], DA, NT)
                    dve.sem_inc(rsab_ready, 1)

            def y_a_tile(t):
                dve.wait_ge(yat_done, t + 1)
                v.tensor_tensor(yT[:, 0:4, t * P:t * P + P], ps[4 + t % 2][:, :].rearrange("p (k t) -> p k t", k=4),
                                goab[:, 0:4].unsqueeze(2).broadcast_to([P, 4, P]), ALU.mult).then_inc(yat_ready, 1)

            def lower_tile(t):
                dve.wait_ge(yahi_ready, t + 1)
                c = slice(t * P, t * P + P)
                v.tensor_tensor(y_lo[:, 0:4, c], yT[:, 0:4, c], y_hi[:, 0:4, c], ALU.subtract).then_inc(yalo_ready, 1)

            y_a_tile(0)
            y_a_tile(1)
            y_b_rows(H // 2 - 1)
            lower_tile(0)
            lower_rows(H // 2 - 1)
            y_a_tile(2)
            lower_tile(1)
            y_a_tile(3)
            lower_tile(2)
            lower_tile(3)
            dve.wait_ge(sb_done, 1)
            v.tensor_copy(ssab[:, 1], ps[6][:, 0:NT]).then_inc(sb_read, 1)
            dve.wait_ge(sb_read, 1)
            rsqrt(rsab[:, 1], ssab[:, 1], DA, NT)
            for t in range(NT):
                for half in range(2):
                    n = 2 * t + half
                    dve.wait_ge(wo_done, n + 1)
                    cols = h[:, t, half * 512:half * 512 + 512]
                    link(v.tensor_tensor(cols, cols, ps[2 * (n % 2)][:, :], ALU.add))
                    v.scalar_tensor_tensor(out=cols, in0=ps[2 * (n % 2) + 1][:, :], scalar=rsab[:, 1, t:t + 1], in1=cols,
                                           op0=ALU.mult, op1=ALU.add).then_inc(h_ready, 1)
                scaled_rows(1, t)
                if t:
                    normed(1, t - 1, hnT[:, :, (t - 1) * P:t * P])
            normed(1, NT - 1, hnT[:, :, (NT - 1) * P:NT * P])
            for b in range(2):
                dve.wait_ge(st_hn[b], 32)
            dve.wait_ge(lg_done, 1)
            link(v.tensor_copy(lg[:, :, :], ps[4][:, 0:NT * (NG + E)].rearrange("p (t n) -> p t n", t=NT)))

            def col(a):
                return a.unsqueeze(2)

            def one_hot_of_max(dst, src, top, n):
                link(v.tensor_reduce(top, src, axis=AX.X, op=ALU.max))
                link(v.tensor_tensor(dst, src, col(top).broadcast_to([P, NT, n]), ALU.is_equal))
                link(v.tensor_tensor(dst, dst, first[:, 0:n].unsqueeze(1).broadcast_to([P, NT, n]), ALU.mult))
                link(v.tensor_reduce(r4[:, :, 3], dst, axis=AX.X, op=ALU.max))
                link(v.tensor_tensor(dst, dst, col(r4[:, :, 3]).broadcast_to([P, NT, n]), ALU.is_equal))

            one_hot_of_max(oh_g[:, :, :], lg[:, :, 0:NG], r4[:, :, 0], NG)
            v.tensor_tensor(lg[:, :, 0:NG], lg[:, :, 0:NG], col(r4[:, :, 0]).broadcast_to([P, NT, NG]), ALU.subtract)\
                .then_inc(ex_in, 1)
            oh_gb = oh_g[:, :, :].unsqueeze(3).broadcast_to([P, NT, NG, EPG])
            l4 = s32[:, :, :].rearrange("p t (g e) -> p t g e", g=NG)
            for t in range(NT):
                link(v.tensor_tensor(l4[:, t], lg[:, t, NG:].rearrange("p (g e) -> p g e", g=NG), oh_gb[:, t], ALU.mult))
            link(v.tensor_reduce(r8[:, :, :], s32[:, :, :].rearrange("p t (g e) -> p t e g", g=NG), axis=AX.X, op=ALU.add))
            one_hot_of_max(oh1[:, :, :], r8[:, :, :], m12[:, 0], EPG)
            link(v.scalar_tensor_tensor(out=t8[:, :, :], in0=oh1[:, :, :], scalar=-BIG, in1=r8[:, :, :],
                                        op0=ALU.mult, op1=ALU.add))
            one_hot_of_max(oh2[:, :, :], t8[:, :, :], m12[:, 1], EPG)
            v.tensor_tensor(m12[:, 1], m12[:, 1], m12[:, 0], ALU.subtract).then_inc(ex_in, 1)
            for t in range(NT):
                for M, oh in ((M1, oh1), (M2, oh2)):
                    link(v.tensor_tensor(M[:, t].rearrange("p (g e) -> p g e", g=NG), oh_gb[:, t],
                                         oh[:, t:t + 1].broadcast_to([P, NG, EPG]), ALU.mult))
            v.tensor_tensor(Mb[:, :, :], M1[:, :, :], M2[:, :, :], ALU.add).then_inc(mb_ready, 1)
            dve.wait_ge(ex_out, 2)
            link(v.tensor_reduce(r4[:, :, 1], lg[:, :, 0:NG], axis=AX.X, op=ALU.add))
            link(v.tensor_scalar(m12[:, 3], m12[:, 2], 1.0, None, ALU.add))
            link(v.tensor_tensor(r4[:, :, 1], r4[:, :, 1], m12[:, 3], ALU.mult))
            link(v.reciprocal(cw[:, 0], r4[:, :, 1]))
            link(v.tensor_tensor(cw[:, 1], cw[:, 0], m12[:, 2], ALU.mult))
            dve.wait_ge(rank_done, 1)
            link(v.tensor_copy(r32[:, :, :], ps[5][:, 0:NT * E].rearrange("p (t e) -> p t e", t=NT)))
            link(v.tensor_copy(Ri[:, :, :], r32[:, :, :]))
            link(v.tensor_copy(cnt[:, :], ps[5][:, NT * E:NT * E + E]))
            link(v.tensor_tensor(cmp8[:, :, :], cnt[:, :].unsqueeze(2).broadcast_to([P, E, EPG]),
                                 n64[:, :].unsqueeze(1).broadcast_to([P, E, EPG]), ALU.is_gt))
            link(v.tensor_reduce(chunks_of[:, :], cmp8[:, :, :], axis=AX.X, op=ALU.add))
            link(v.tensor_reduce(nr[:, :], chunks_of[:, :].rearrange("p (q b) -> p q b", b=2), axis=AX.X, op=ALU.max))
            link(v.tensor_scalar(nr[:, :], nr[:, :], 1.0, None, ALU.max))
            link(v.tensor_tensor_scan(out=incl[:, :], data0=nr[:, :], data1=nr[:, :], initial=0.0,
                                      op0=ALU.add, op1=ALU.max))
            link(v.tensor_tensor(base[:, :], incl[:, :], nr[:, :], ALU.subtract))
            link(v.scalar_tensor_tensor(out=z0[:, :].rearrange("p (q b) -> p q b", b=2),
                                        in0=base[:, :].unsqueeze(2).broadcast_to([P, NPAIR, 2]), scalar=float(P),
                                        in1=odd64[:, :, :], op0=ALU.mult, op1=ALU.add))
            link(v.tensor_scalar(Fi[:, :, :], Ri[:, :, :], 6, None, ALU.logical_shift_right))
            link(v.tensor_scalar(Ri[:, :, :], Ri[:, :, :], BLK - 1, None, ALU.bitwise_and))
            link(v.scalar_tensor_tensor(out=r32[:, :, :], in0=Fi[:, :, :], scalar=float(P), in1=Ri[:, :, :],
                                        op0=ALU.mult, op1=ALU.add))
            link(v.tensor_tensor(r32[:, :, :], r32[:, :, :], z0[:, :].unsqueeze(1).broadcast_to([P, NT, E]), ALU.add))
            for k, M in ((0, M1), (1, M2)):
                link(v.tensor_tensor(s32[:, :, :], M[:, :, :], r32[:, :, :], ALU.mult))
                link(v.tensor_reduce(posf[:, k], s32[:, :, :], axis=AX.X, op=ALU.add))
            link(v.tensor_copy(posi[:, :, :], posf[:, :, :]))
            link(v.tensor_scalar(rndi[:, :, :], posi[:, :, :], 7, None, ALU.logical_shift_right))
            link(v.tensor_scalar(posi[:, :, :], posi[:, :, :], P - 1, None, ALU.bitwise_and))
            link(v.tensor_copy(rndf[:, :], rndi[:, :, :].rearrange("p k t -> p (k t)")))
            link(v.tensor_copy(rowf[:, :], posi[:, :, :].rearrange("p k t -> p (k t)")))
            link(v.tensor_tensor(ohb[:, :, :], slf[:, 0:NR].unsqueeze(1).broadcast_to([P, 2 * NT, NR]),
                                 rndf[:, :].unsqueeze(2).broadcast_to([P, 2 * NT, NR]), ALU.is_equal))
            link(v.tensor_tensor(ohb[:, :, :], ohb[:, :, :], rowv[:, :, :].rearrange("p k t -> p (k t)").unsqueeze(2)
                                 .broadcast_to([P, 2 * NT, NR]), ALU.mult))
            v.tensor_tensor(ohs[:, :, :], slf[:, :].unsqueeze(1).broadcast_to([P, 2 * NT, P]),
                            rowf[:, :].unsqueeze(2).broadcast_to([P, 2 * NT, P]), ALU.is_equal).then_inc(oh_ready, 1)
            link(v.tensor_copy(regf[:, 0:NPAIR], nr[:, :]))
            link(v.tensor_scalar(regf[:, NPAIR:2 * NPAIR], base[:, :], 2.0, None, ALU.mult))
            for n in range(2):
                link(v.tensor_scalar(regf[:, (2 + n) * NPAIR:(3 + n) * NPAIR], incl[:, :], 2.0, n + 1.0, ALU.mult,
                                     ALU.add))
            link(v.tensor_copy(regf[:, 4 * NPAIR:4 * NPAIR + 1], incl[:, NPAIR - 1:NPAIR]))
            link(v.tensor_copy(regs[:, :], regf[:, :]))
            dve.wait_ge(idx_done, 1)
            link(v.tensor_scalar(tbl[:, :], ps[6][:, 0:NR], -1.0, 0.0, ALU.add, ALU.max))
            link(v.tensor_scalar(tb2[:, :], ps[6][:, 0:NR], float(S), float(-S), ALU.is_gt, ALU.mult))
            link(v.tensor_tensor(tb2[:, :], tbl[:, :], tb2[:, :], ALU.add))
            link(v.tensor_scalar(none[:, :], ps[6][:, 0:NR], 0.0, float(4 * PAIRS), ALU.is_equal, ALU.mult))
            link(v.tensor_tensor(gidx[:, :], tb2[:, :], none[:, :], ALU.add))
            v.tensor_tensor(sidx[:, :], tbl[:, :], none[:, :], ALU.add).then_inc(idx_ready, 1)
            dve.wait_ge(idx_ready, 1)
            rounds = dve.value_load(regs[0:1, 4 * NPAIR:4 * NPAIR + 1], min_val=NPAIR, max_val=NR - 1)

            def xgt_copy(m, half):
                dve.wait_ge(xgt_done, m)
                v.tensor_tensor(xgT[:, 4 * half:4 * half + 4], ps[6 + half][:, :].rearrange("p (k s) -> p k s", k=4),
                                g3[:, 1, 4 * half:4 * half + 4].unsqueeze(2).broadcast_to([P, 4, P]), ALU.mult)\
                    .then_inc(xgt_ready, 1)

            for half in range(2):
                xgt_copy(half + 1, half)
            with dve.Fori(0, rounds) as r:
                for s in range(2):
                    dve.wait_ge(sil_ready, 2 * r + (s + 1))
                    dve.wait_ge(at_done, 2 * r + (s + 1))
                    v.tensor_tensor(act[:, s], sil[:, s], ps[s][:, P:2 * P], ALU.mult).then_inc(act_ready, 1)
                for s in range(2):
                    dve.wait_ge(at_done, 2 * r + (s + 3))
                    dve.wait_ge(block_done, 2 * r + (s + 1))
                    v.tensor_copy(aT[:, s], ps[4][:, s * P:s * P + P]).then_inc(at_ready, 1)
                    xgt_copy(2 * r + (s + 3), s)
            def combine(t):
                dve.wait_ge(ld_yg[t % 2], 16 * (t // 2 + 1))
                for k in range(2):
                    v.scalar_tensor_tensor(out=h[:, t], in0=yg[t % 2][:, k], scalar=cw[:, k, t:t + 1], in1=h[:, t],
                                           op0=ALU.mult, op1=ALU.add).then_inc(h2_ready, 1)
                    dve.wait_ge(h2_ready, 2 * t + k + 1)

            def finish(t):
                for half in range(2):
                    n = 2 * t + half
                    dve.wait_ge(sg_ready, n + 1)
                    c = slice(half * 512, half * 512 + 512)
                    v.tensor_tensor(pW[:, t, c], pW[:, t, c], sg[:, n % 2], ALU.mult).then_inc(sg_used, 1)
                    dve.wait_ge(sg_used, n + 1)
                    last = v.tensor_tensor(h[:, t, c], h[:, t, c], pW[:, t, c], ALU.add)
                    if half == 0:
                        link(last)
                last.then_inc(out_ready, 1)


            def lower_gate(half):
                c = slice(half * 512, half * 512 + 512)
                for k in range(0, KD, 2):
                    dve.wait_ge(pghi_ready, 4 * half + k // 2 + 1)
                    v.tensor_tensor(wpg_lo[:, k:k + 2, c], wpg[:, k:k + 2, c], wpg_hi[:, k:k + 2, c], ALU.subtract)\
                        .then_inc(pglo_ready, 1)

            lower_gate(0)
            combine(0)
            scaled_rows(2, 0)
            combine(1)
            for t in range(NT):
                if t >= 2:
                    dve.wait_ge(pg_done, 2 * (t - 1))
                normed(2, t, hpT[:, t % 2])
                dve.wait_ge(hphi_ready, t + 1)
                v.tensor_tensor(hp_lo[:, t % 2], hpT[:, t % 2], hp_hi[:, t % 2], ALU.subtract).then_inc(hplo_ready, 1)
                if t == 0:
                    lower_gate(1)
                if t + 1 < NT:
                    scaled_rows(2, t + 1)
                if t + 2 < NT:
                    combine(t + 2)
                if t:
                    finish(t - 1)
            finish(NT - 1)


_INS = ["x", "p", "g_mix", "w_in", "g_v_a", "w_s", "b_s", "g_q", "g_k", "g_out_a", "g_out_b", "w_out", "g_ffn",
        "w_group", "w_expert", "w_gate_e", "w_up_e", "w_down_e", "g_ple", "w_ple", "w_ple_gate"]


def kernel(**inputs):
    import numpy as np
    import concourse.bacc as bacc
    from concourse.bass_utils import run_bass_kernel_spmd

    nc = bacc.Bacc("TRN2", target_bir_lowering=False, num_devices=1)
    arrays, args = {}, []
    for name in _INS:
        a = np.ascontiguousarray(inputs[name])
        arrays[f"in_{name}"] = a
        args.append(nc.dram_tensor(f"in_{name}", a.shape, mybir.dt.from_np(a.dtype), kind="ExternalInput").ap())
    out = nc.dram_tensor("out_h", (1, S, D), F32, kind="ExternalOutput").ap()
    hybrid_layer(nc, *args, out)
    r = run_bass_kernel_spmd(nc, [arrays], core_ids=[0])
    return r.results[0]["out_h"]
```
